# Optimizing a Trainium2 kernel written in Bass

```python
import math
import jax, jax.numpy as jnp
from jax import lax
import numpy as np

D_MODEL = 1024
BATCH = 1
SEQ = 256
DEPTH = 1
DEC_BATCH = 1
DEC_SEQ = 512
PAST_LEN = 128

POOL_WINDOWS = (2, 4, 8, 16)
N_POOL_GROUPS = 4
POOL_GROUP_DIM = D_MODEL // 8
POOL_DIM = N_POOL_GROUPS * POOL_GROUP_DIM
N_ATT_HEADS = 8
ATT_HEAD_DIM = D_MODEL // (2 * N_ATT_HEADS)
ATT_V_DIM = 2 * ATT_HEAD_DIM
ATT_DIM = N_ATT_HEADS * ATT_V_DIM
QKV_DIM = 3 * ATT_DIM
IN_DIM = POOL_DIM + QKV_DIM
ROPE_THETA = 10000.0
Q_BLOCK = 128
N_BRANCHES = 2
PEER_HEADS = 8
PEER_KEYS = 128
PEER_EXPERTS = PEER_KEYS * PEER_KEYS
PEER_TOPK = 16
PEER_KEY_DIM = 128
PEER_HALF = PEER_KEY_DIM // 2
TOKEN_CHUNK = 128
NORM_EPS = 1e-6

kernel_name = "hybrid_pool_diffattn_peer_encoder"

def _rmsnorm(x, g):
    xf = x.astype(jnp.float32)
    y = xf * lax.rsqrt(jnp.mean(xf * xf, axis=-1, keepdims=True) + NORM_EPS)
    return (y * g.astype(jnp.float32)).astype(x.dtype)

def _rope_tables(S, dtype):
    inv_freq = 1.0 / (ROPE_THETA ** (jnp.arange(0, ATT_HEAD_DIM, 2, dtype=jnp.float32) / ATT_HEAD_DIM))
    ang = jnp.arange(S, dtype=jnp.float32)[:, None] * inv_freq[None, :]
    ang = jnp.concatenate([ang, ang], axis=-1)[:, None, :]
    return jnp.cos(ang).astype(dtype), jnp.sin(ang).astype(dtype)

def _apply_rope(t, cos, sin):
    t1, t2 = jnp.split(t, 2, axis=-1)
    return t * cos + jnp.concatenate([-t2, t1], axis=-1) * sin

def _multiscale_pool(p, pool_w, pool_scale):
    B, S, _ = p.shape
    pg = p.reshape(B, S, N_POOL_GROUPS, POOL_GROUP_DIM)
    csum = jnp.cumsum(pg.astype(jnp.float32), axis=1)
    csum = jnp.concatenate([jnp.zeros_like(csum[:, :1]), csum], axis=1)
    pos = jnp.arange(S, dtype=jnp.int32)[None, :]
    win = jnp.asarray(POOL_WINDOWS, dtype=jnp.int32)[:, None]
    lo = jnp.clip(pos - win // 2, 0, S)
    hi = jnp.clip(pos + win - win // 2, 0, S)
    gidx = jnp.arange(N_POOL_GROUPS, dtype=jnp.int32)[:, None]
    wsum = csum[:, hi, gidx] - csum[:, lo, gidx]
    cnt = (hi - lo).astype(jnp.float32)[None, :, :, None]
    mean = jnp.transpose(wsum / cnt, (0, 2, 1, 3)).astype(p.dtype)
    mixed = jnp.einsum('bsgc,gce->bsge', mean - pg, pool_w)
    return mixed.reshape(B, S, POOL_DIM) * pool_scale

def _diff_attention(qkv, cos, sin, lam, g_sub, lam_init):
    B, S, _ = qkv.shape
    q, k, v = jnp.split(qkv, 3, axis=-1)
    q = _apply_rope(q.reshape(B, S, 2 * N_ATT_HEADS, ATT_HEAD_DIM), cos, sin)
    k = _apply_rope(k.reshape(B, S, 2 * N_ATT_HEADS, ATT_HEAD_DIM), cos, sin)
    v = v.reshape(B, S, N_ATT_HEADS, ATT_V_DIM)
    nb = S // Q_BLOCK
    qb = jnp.transpose(q.reshape(B, nb, Q_BLOCK, 2 * N_ATT_HEADS, ATT_HEAD_DIM), (1, 0, 2, 3, 4))
    scale = ATT_HEAD_DIM ** -0.5

    def block(q_blk):
        s = jnp.einsum('bqhd,bkhd->bhqk', q_blk, k).astype(jnp.float32) * scale
        pr = jax.nn.softmax(s, axis=-1).reshape(B, N_ATT_HEADS, 2, Q_BLOCK, S)
        a = pr[:, :, 0] - lam * pr[:, :, 1]
        return jnp.einsum('bhqk,bkhe->bqhe', a.astype(v.dtype), v)

    o = lax.map(block, qb)
    o = jnp.transpose(o, (1, 0, 2, 3, 4)).reshape(B, S, N_ATT_HEADS, ATT_V_DIM)
    o = _rmsnorm(o, g_sub) * (1.0 - lam_init)
    return o.reshape(B, S, ATT_DIM)

def _peer(h, w_q, keys, u_tab, v_tab):
    B, S, D = h.shape
    hc = h.reshape(-1, TOKEN_CHUNK, D)

    def chunk(xc):
        q = (xc @ w_q).reshape(TOKEN_CHUNK, PEER_HEADS, 2, PEER_HALF)
        s = jnp.einsum('thpd,hpnd->thpn', q, keys).astype(jnp.float32)
        top_s, top_i = lax.top_k(s, PEER_TOPK)
        cand = top_s[:, :, 0, :, None] + top_s[:, :, 1, None, :]
        best_s, best_j = lax.top_k(cand.reshape(TOKEN_CHUNK, PEER_HEADS, PEER_TOPK * PEER_TOPK), PEER_TOPK)
        i1 = jnp.take_along_axis(top_i[:, :, 0], best_j // PEER_TOPK, axis=-1)
        i2 = jnp.take_along_axis(top_i[:, :, 1], best_j % PEER_TOPK, axis=-1)
        expert = i1 * PEER_KEYS + i2
        g = jax.nn.softmax(best_s, axis=-1)
        u = jnp.take(u_tab, expert, axis=0)
        act = jax.nn.gelu(jnp.einsum('thkd,td->thk', u, xc).astype(jnp.float32), approximate=False) * g
        vv = jnp.take(v_tab, expert, axis=0)
        return jnp.einsum('thk,thkd->td', act.astype(vv.dtype), vv)

    return lax.map(chunk, hc).reshape(B, S, D)

def _trunk(x, c, w_ada, b_ada, g_norm1, w_in, pool_w, pool_scale, w_pool_out,
           lam_q1, lam_k1, lam_q2, lam_k2, g_sub, w_att_out, w_gate, b_gate, w_out,
           g_norm2, w_peer_q, peer_keys, peer_u, peer_v, g_final):
    B, S, D = x.shape
    cos, sin = _rope_tables(S, x.dtype)
    for l in range(DEPTH):
        lam_init = 0.8 - 0.6 * math.exp(-0.3 * l)
        mod = jax.nn.silu(c) @ w_ada[l] + b_ada[l]
        sh1, sc1, gt1, sh2, sc2, gt2 = [m[:, None, :] for m in jnp.split(mod, 6, axis=-1)]
        h = _rmsnorm(x, g_norm1[l]) * (1 + sc1) + sh1
        proj = h @ w_in[l]
        y_pool = _multiscale_pool(proj[..., :POOL_DIM], pool_w[l], pool_scale[l]) @ w_pool_out[l]
        lam = (jnp.exp(jnp.sum(lam_q1[l].astype(jnp.float32) * lam_k1[l].astype(jnp.float32)))
               - jnp.exp(jnp.sum(lam_q2[l].astype(jnp.float32) * lam_k2[l].astype(jnp.float32)))
               + lam_init)
        y_att = _diff_attention(proj[..., POOL_DIM:], cos, sin, lam, g_sub[l], lam_init) @ w_att_out[l]
        gates = jax.nn.sigmoid(h @ w_gate[l] + b_gate[l])
        g_pool, g_att = jnp.split(gates, N_BRANCHES, axis=-1)
        x = x + gt1 * ((g_pool * y_pool + g_att * y_att) @ w_out[l])
        h2 = _rmsnorm(x, g_norm2[l]) * (1 + sc2) + sh2
        x = x + gt2 * _peer(h2, w_peer_q[l], peer_keys[l], peer_u[l], peer_v[l])
    return _rmsnorm(x, g_final)

def setup_inputs(seed: int = 0) -> dict:
    key = jax.random.key(seed)
    ks = jax.random.split(key, 32)
    f32 = jnp.float32
    nrm = lambda k, shape, s: jax.random.normal(k, shape, dtype=f32) * s
    L, D = DEPTH, D_MODEL
    return {
        "x_prompt": nrm(ks[0], (BATCH, SEQ, D), 1.0),
        "x_sample": nrm(ks[1], (DEC_BATCH, DEC_SEQ, D), 1.0),
        "c_prompt": nrm(ks[2], (BATCH, D), 1.0),
        "c_sample": nrm(ks[3], (DEC_BATCH, D), 1.0),
        "w_ada": nrm(ks[4], (L, D, 6 * D), D ** -0.5),
        "b_ada": nrm(ks[5], (L, 6 * D), 0.02),
        "g_norm1": 1.0 + nrm(ks[6], (L, D), 0.02),
        "w_in": nrm(ks[7], (L, D, IN_DIM), D ** -0.5),
        "pool_w": nrm(ks[8], (L, N_POOL_GROUPS, POOL_GROUP_DIM, POOL_GROUP_DIM), POOL_GROUP_DIM ** -0.5),
        "pool_scale": 1.0 + nrm(ks[9], (L, POOL_DIM), 0.1),
        "w_pool_out": nrm(ks[10], (L, POOL_DIM, D), POOL_DIM ** -0.5),
        "lam_q1": nrm(ks[11], (L, ATT_HEAD_DIM), 0.1),
        "lam_k1": nrm(ks[12], (L, ATT_HEAD_DIM), 0.1),
        "lam_q2": nrm(ks[13], (L, ATT_HEAD_DIM), 0.1),
        "lam_k2": nrm(ks[14], (L, ATT_HEAD_DIM), 0.1),
        "g_sub": 1.0 + nrm(ks[15], (L, ATT_V_DIM), 0.02),
        "w_att_out": nrm(ks[16], (L, ATT_DIM, D), ATT_DIM ** -0.5),
        "w_gate": nrm(ks[17], (L, D, N_BRANCHES * D), D ** -0.5),
        "b_gate": nrm(ks[18], (L, N_BRANCHES * D), 0.02),
        "w_out": nrm(ks[19], (L, D, D), D ** -0.5),
        "g_norm2": 1.0 + nrm(ks[20], (L, D), 0.02),
        "w_peer_q": nrm(ks[21], (L, D, PEER_HEADS * PEER_KEY_DIM), D ** -0.5),
        "peer_keys": nrm(ks[22], (L, PEER_HEADS, 2, PEER_KEYS, PEER_HALF), PEER_HALF ** -0.5),
        "peer_u": nrm(ks[23], (L, PEER_EXPERTS, D), D ** -0.5),
        "peer_v": nrm(ks[24], (L, PEER_EXPERTS, D), PEER_HEADS ** -0.5),
        "g_final": 1.0 + nrm(ks[25], (D,), 0.02),
    }

def reference(x_prompt, x_sample, c_prompt, c_sample, w_ada, b_ada, g_norm1, w_in, pool_w,
              pool_scale, w_pool_out, lam_q1, lam_k1, lam_q2, lam_k2, g_sub, w_att_out,
              w_gate, b_gate, w_out, g_norm2, w_peer_q, peer_keys, peer_u, peer_v, g_final):
    y_prompt = _trunk(x_prompt, c_prompt, w_ada, b_ada, g_norm1, w_in, pool_w, pool_scale,
                      w_pool_out, lam_q1, lam_k1, lam_q2, lam_k2, g_sub, w_att_out, w_gate,
                      b_gate, w_out, g_norm2, w_peer_q, peer_keys, peer_u, peer_v, g_final)
    y_sample = _trunk(x_sample, c_sample, w_ada, b_ada, g_norm1, w_in, pool_w, pool_scale,
                      w_pool_out, lam_q1, lam_k1, lam_q2, lam_k2, g_sub, w_att_out, w_gate,
                      b_gate, w_out, g_norm2, w_peer_q, peer_keys, peer_u, peer_v, g_final)
    return (y_prompt, y_sample)


_drawn_inputs = setup_inputs


def setup_inputs(seed=0):
    import zlib

    import numpy as np

    out = dict(_drawn_inputs(seed))
    spreads = {}
    factors = {'g_norm1': 3.728,
     'lam_k1': 3.525,
     'lam_q2': 3.7,
     'lam_k2': 4.762,
     'g_sub': 15.879,
     'b_gate': 7.79,
     'g_norm2': 9.541,
     'g_final': 7.405}
    for name, (base, spread) in spreads.items():
        noise = np.random.default_rng([zlib.crc32(name.encode()), seed]).standard_normal(out[name].shape)
        drawn = base * np.exp(spread * noise) if base else spread * noise
        out[name] = __import__('jax').numpy.asarray(drawn.astype(out[name].dtype))
    for name, factor in factors.items():
        out[name] = (out[name] * factor).astype(out[name].dtype)
    return out
```

```python
from contextlib import ExitStack

import numpy as np

import concourse.bass as bass
from concourse import mybir

F32 = mybir.dt.float32
U32 = mybir.dt.uint32
ALU = mybir.AluOpType
ACT = mybir.ActivationFunctionType
AX = mybir.AxisListType

P = 128
D = 1024
KC = D // P
HEADS = 8
HALF = 64
TOPK = 16
SEQS = (256, 512)
SMAX = max(SEQS)
EPS = 1e-6
LAM_INIT = 0.2
WINDOWS = (2, 4, 8, 16)
PAD = 8
LROW = SMAX + 2 * PAD
TOK = 256
TILE = KC * P
UNIT = 4 * TILE
UNITS_ADA = 12
UNITS_GROUP = 21
NEG = -3.0e38

C_ID, C_ONE, C_ROT, C_IOTA, C_EDGE, C_N = 0, 128, 256, 384, 512, 512 + 4 * 16
V_G1, V_G2, V_BADA, V_BGATE, V_PSC, V_GSUB, V_C, V_LAM, V_N = 0, 8, 16, 64, 80, 84, 85, 101, 101 + 4 * 64


def after(eng, sem, n):
    if isinstance(n, int) and n <= 0:
        return
    eng.wait_ge(sem, n)


def build(nc, consts, params, rope, keys, pool_w, g_final, x_t, weights, table, outs):
    with ExitStack() as ctx:
        def sb(name, shape, dt=F32):
            return ctx.enter_context(nc.sbuf_tensor(name, shape, dt))

        def sem(name):
            return ctx.enter_context(nc.semaphore(name))

        x1_dram = nc.dram_tensor("x1_scratch", (sum(SEQS) // P, P, D), F32, kind="Internal").ap()

        cst = sb("cst", [P, C_N])
        par = sb("par", [P, V_N])
        ident, ones, rot = cst[:, C_ID:C_ID + P], cst[:, C_ONE:C_ONE + P], cst[:, C_ROT:C_ROT + P]
        iota = cst[:, C_IOTA:C_IOTA + P]
        edge = cst[:, C_EDGE:C_EDGE + 64].rearrange("p (g n) -> p g n", g=4)
        mod = sb("mod", [P, 48, 2])
        scl = sb("scl", [P, 2, 2, KC])
        silu_c = sb("silu_c", [P, KC, 2])
        small = sb("small", [P, 16])
        gsub = sb("gsub", [P, 1])
        nlam = sb("nlam", [P, 1])
        h2 = sb("h2", [P, KC, SMAX])
        sel_t = sb("sel_t", [P, 3, SMAX])
        ring = sb("ring", [P, 2 * UNIT])
        onehot = sb("onehot", [P, 2, 2, 4, P])
        coef = sb("coef", [P, 2, TOK])
        gel = sb("gel", [P, 2, TOK])
        arena = sb("arena", [P, P * TOK])

        place = [0]

        def lay(*dims):
            n = int(np.prod(dims))
            a = arena[:, place[0]:place[0] + n]
            place[0] += n
            names = "abcd"[:len(dims)]
            if len(dims) > 1:
                a = a.rearrange("p (%s) -> p %s" % (" ".join(names), " ".join(names)),
                                **{k: v for k, v in zip(names, dims)})
            return a

        gates = arena[:, :].rearrange("p (j t) -> p j t", j=P)
        hbuf = lay(KC, SMAX)
        obuf = lay(KC, SMAX)
        zbuf = lay(KC, SMAX)
        pbuf = lay(4, LROW)
        ptmp = lay(2, LROW)
        pdif = lay(4, SMAX)
        qk = lay(2, 2, SMAX)
        qkraw = lay(2, SMAX)
        rtmp = lay(SMAX)
        vh = lay(2, SMAX)
        expd = lay(2, 2, SMAX)
        amix = lay(2, SMAX)
        amix_t = lay(4, SMAX)
        sq = lay(2, SMAX)
        rstd = lay(SMAX)
        orstd = (rstd, rtmp)
        cossin = lay(2, SMAX)
        poolw = lay(4, P)
        assert place[0] <= P * TOK, place
        base_topk = 2 * KC * SMAX
        place[0] = base_topk
        keybd = lay(HEADS, 2 * P)
        qh = lay(2, SMAX)
        place[0] = base_topk + KC * SMAX
        sc = lay(2, 4 * 2 * P)
        sc2 = lay(2 * P)
        best = lay(4, 2, TOPK)
        besti = lay(4, 2, TOPK)
        bestf = lay(4, 2, TOPK)
        cand = lay(TOPK, TOPK)
        cand2 = lay(TOPK, TOPK)
        jbest = lay(TOPK)
        jhalf = lay(2, TOPK)
        jf = lay(2, TOPK)
        mask = lay(2, TOPK, TOPK)
        sel = lay(4, 3, P)
        gsum = lay(4 * HEADS)
        x1tok = lay(2, D)
        place[0] = 0
        f_gt2, f_gf, f_x1, f_y, f_sq = lay(D), lay(D), lay(2, D), lay(2, D), lay(D)
        f_diag = lay(2, P)

        ps = ctx.enter_context(nc.psum_tensor("ps", [P, 8, 512], F32))

        consts_in = sem("consts_in")
        group_in = sem("group_in")
        phase = sem("phase")
        unit_in = [sem("unit_in0"), sem("unit_in1")]
        silu_a, silu_b, ada_done = sem("silu_a"), sem("silu_b"), sem("ada_done")
        lam_dot, lam_exp = sem("lam_dot"), sem("lam_exp")
        sq_ready, sq_summed, var_ready, rstd_ready, norm_done = (
            sem("sq_ready"), sem("sq_summed"), sem("var_ready"), sem("rstd_ready"), sem("norm_done"))
        p_done, p_copied, pool_pad, pool_diff = sem("p_done"), sem("p_copied"), sem("pool_pad"), sem("pool_diff")
        mix_done, mix_copied = sem("mix_done"), sem("mix_copied")
        proj = {k: sem(k + "_proj") for k in "qkv"}
        copied = {k: sem(k + "_copied") for k in "qkv"}
        rotated = {k: sem(k + "_rotated") for k in "qk"}
        roped = {k: sem(k + "_roped") for k in "qk"}
        scored, maxed, expd_ready, mixed, turned, turned_copied = (
            sem("scored"), sem("maxed"), sem("expd_ready"), sem("mixed"), sem("turned"), sem("turned_copied"))
        pv_done, o_copied = sem("pv_done"), sem("o_copied")
        z_done, sig_done, z_ready = sem("z_done"), sem("sig_done"), sem("z_ready")
        out_done, x1_ready, x_again = sem("out_done"), sem("x1_ready"), sem("x_again")
        x1_turned, x1_copied, x1_stored = sem("x1_turned"), sem("x1_copied"), [sem("x1_stored0"), sem("x1_stored1")]
        keys_in, pq_done, pq_copied, keyed, keyed_copied, searched = (
            sem("keys_in"), sem("pq_done"), sem("pq_copied"), sem("keyed"), sem("keyed_copied"), sem("searched"))
        shifted, exped, sel_ready, sel_turned, sel_copied = (
            sem("shifted"), sem("exped"), sem("sel_ready"), sem("sel_turned"), sem("sel_copied"))
        hot_ready, g_done, g_copied = sem("hot_ready"), sem("g_done"), sem("g_copied")
        o_normed = sem("o_normed")
        tile_in = [sem("tile_in%d" % i) for i in range(4)]
        s_done, gelu_done, coef_ready, v_done = sem("s_done"), sem("gelu_done"), sem("coef_ready"), sem("v_done")
        fin_in, diag_ready, gt2_done, gt2_copied = sem("fin_in"), sem("diag_ready"), sem("gt2_done"), sem("gt2_copied")
        y_ready, y_squared, y_var, y_rstd, y_final, y_stored = (
            sem("y_ready"), sem("y_squared"), sem("y_var"), sem("y_rstd"), sem("y_final"), sem("y_stored"))

        block = ctx.enter_context(nc.Block())

        phases = {}

        def all_done(eng):
            n = phases[id(eng)] = phases.get(id(eng), 0) + 1
            eng.drain()
            eng.sem_inc(phase, 1)
            eng.wait_ge(phase, 5 * n)

        def wtile(u, i):
            o = (u % 2) * UNIT + i * TILE
            return ring[:, o:o + TILE].rearrange("p (k n) -> p k n", k=KC)

        def unit_landed(eng, u):
            eng.wait_ge(unit_in[u % 2], 16 * (u // 2 + 1))

        def exp_tile(slot):
            t = ring[:, slot * 2 * D:(slot + 1) * 2 * D]
            return t[:, 0:D].rearrange("p (k n) -> p k n", k=KC), t[:, D:2 * D]

        ubase = [UNITS_ADA + g * UNITS_GROUP for g in range(2)]
        qbase = [0, HEADS * SEQS[0] // P]
        passes = [1, 2]
        pbase = [0, 1]
        tbase = [0, SEQS[0] // P]

        @block.sync
        def _(sp):
            sp.dma_start(par[:], params).then_inc(consts_in, 16)
            sp.dma_start(cst[:], consts).then_inc(consts_in, 16)

            def load_unit(u, half):
                sp.dma_start(ring[:, half * UNIT:(half + 1) * UNIT], u).then_inc(unit_in[half], 16)

            def weight_unit(u):
                return weights[bass.ds(u, 1)].rearrange("a p n -> (a p) n")

            for u in range(2):
                load_unit(weights[u], u)
            with sp.Fori(1, UNITS_ADA // 2) as i:
                for j in range(2):
                    sp.wait_ge(ada_done, 2 * i + j - 1)
                    load_unit(weight_unit(2 * i + j), j)
            for g, S in enumerate(SEQS):
                if g:
                    all_done(sp)
                sp.dma_start(hbuf[:, :, 0:S], x_t[g]).then_inc(group_in, 16)
                sp.dma_start(cossin[:, :, 0:S], rope[:, :, 0:S]).then_inc(group_in, 16)
                sp.dma_start(poolw, pool_w).then_inc(group_in, 16)
                b = ubase[g]

                def load(n, used, count):
                    sp.wait_ge(used, count)
                    load_unit(weights[UNITS_ADA + n], (b + n) % 2)

                load(0, ada_done, UNITS_ADA - 1)
                load(1, ada_done, UNITS_ADA)
                load(2, p_done, 4 * g + 4)
                with sp.Fori(1, HEADS // 2) as i:
                    for j in range(2):
                        sp.wait_ge(proj["v"], 2 * i + (8 * g + j - 1))
                        load_unit(weight_unit(2 * i + (UNITS_ADA + 1 + j)), (b + 1 + j) % 2)
                load(9, proj["v"], 8 * g + 7)
                load(10, proj["v"], 8 * g + 8)
                with sp.Fori(1, KC // 2) as i:
                    for j in range(2):
                        sp.wait_ge(z_done, 2 * i + (8 * g + j - 1))
                        load_unit(weight_unit(2 * i + (UNITS_ADA + 9 + j)), (b + 9 + j) % 2)
                load(17, z_done, 8 * g + 7)
                load(18, z_done, 8 * g + 8)
                sp.wait_ge(z_done, HEADS * (g + 1))
                sp.dma_start(obuf[:, :, 0:S], x_t[g]).then_inc(x_again, 16)
                load(19, out_done, 8 * g + 4)
                load(20, out_done, 8 * g + 8)
                sp.dma_start(keybd, keys).then_inc(keys_in, 16)
                for tb in range(S // P):
                    sp.wait_ge(x1_copied, tbase[g] + tb + 1)
                    sp.dma_start(x1_dram[tbase[g] + tb], x1tok[:, tb % 2, :]).then_inc(x1_stored[tb % 2], 16)
                for j in range(2):
                    sp.wait_ge(x1_stored[j], 16 * (tbase[g] + S // P) // 2)
                all_done(sp)
                for n in range(passes[g]):
                    pp = pbase[g] + n
                    if n:
                        all_done(sp)
                    for t in range(4):
                        sp.dma_start(ring[:, t * 2 * D:(t + 1) * 2 * D], table[t]).then_inc(tile_in[t], 16)
                    with sp.Fori(1, P // 4) as i:
                        for t in range(4):
                            sp.wait_ge(v_done, 4 * i + (pp * P + t - 3))
                            sp.dma_start(ring[:, t * 2 * D:(t + 1) * 2 * D],
                                         table[bass.ds(4 * i + t, 1)].rearrange("a p n -> (a p) n")
                                         ).then_inc(tile_in[t], 16)
                    sp.wait_ge(coef_ready, (pp + 1) * P)
                    sp.dma_start(f_gf, g_final).then_inc(fin_in, 16)
                    for j in range(2):
                        sp.dma_start(f_x1[:, j, :], x1_dram[tbase[g] + 2 * n + j]).then_inc(fin_in, 16)
                    for j in range(2):
                        sp.wait_ge(y_final, 2 * pp + j + 1)
                        r = n * TOK + j * P
                        sp.dma_start(outs[g][0, r:r + P, :], f_y[:, j, :]).then_inc(y_stored, 16)
                    sp.wait_ge(y_stored, 32 * (pp + 1))

        @block.tensor
        def _(pe):
            mm = nc.tensor.matmul
            pe.wait_ge(consts_in, 32)
            pe.wait_ge(silu_b, 1)
            with pe.Fori(0, UNITS_ADA // 2) as u2:
                for j in range(2):
                    pe.wait_ge(unit_in[j], 16 * u2 + 16)
                    for i in range(4):
                        for k in range(KC):
                            last = mm(ps[:, 0, bass.ds(16 * u2 + (8 * j + 2 * i), 2)], wtile(j, i)[:, k, :],
                                      silu_c[:, k, :], start=(k == 0), stop=(k == KC - 1))
                    last.then_inc(ada_done, 1)

            for g, S in enumerate(SEQS):
                B = S // P
                b = ubase[g]
                if g:
                    all_done(pe)

                def sum_squares(n0):
                    for c in range(KC):
                        pe.wait_ge(sq_ready, n0 + c + 1)
                        mm(ps[:, 2, 0:S], ones, sq[:, c % 2, 0:S], start=(c == 0),
                           stop=(c == KC - 1)).then_inc(sq_summed, 1)

                def product(bank, w, src, n=KC):
                    for k in range(n):
                        last = mm(ps[:, bank, 0:S], w[:, k, :], src[:, k, 0:S], start=(k == 0), stop=(k == n - 1))
                    return last

                nsq = g * 24
                pe.wait_ge(group_in, 48 * (g + 1))
                sum_squares(nsq)
                pe.wait_ge(norm_done, 2 * g + 1)

                unit_landed(pe, b)
                for c in range(4):
                    n = 4 * g + c
                    if c >= 2:
                        pe.wait_ge(p_copied, n - 1)
                    product(c % 2, wtile(b, c), hbuf).then_inc(p_done, 1)
                pe.wait_ge(p_copied, 4 * g + 4)

                def head(h, par_, do_proj, do_att):
                    hg = 8 * g + h
                    u = b + 1 + par_
                    w = wtile(u, 0), wtile(u, 1), wtile(u, 2)
                    q0 = qbase[g] + (h - 1) * B

                    def scores(j):
                        if j == 0:
                            for x in "qk":
                                after(pe, roped[x], hg)
                        after(pe, expd_ready, q0 + j)
                        o = 1 - par_
                        for m in range(2):
                            r = slice(HALF * m, HALF * m + HALF)
                            last = mm(ps[:, 3 + m, 0:S], qk[r, o, 0, j * P:(j + 1) * P], qk[r, o, 1, 0:S],
                                      start=True, stop=True)
                        last.then_inc(scored, 1)

                    def turn(j):
                        pe.wait_ge(mixed, q0 + j + 1)
                        after(pe, turned_copied, q0 + j)
                        for kb in range(B):
                            last = nc.tensor.transpose(ps[:, 5, kb * P:(kb + 1) * P],
                                                       amix[:, j % 2, kb * P:(kb + 1) * P], ident)
                        last.then_inc(turned, 1)

                    def project(x, i, bank, free_sem, free_n):
                        after(pe, free_sem, free_n)
                        if i == 0:
                            pe.wait_ge(unit_in[u % 2], 16 * (u // 2 + 1) + 8 * (h - par_))
                        if x != "v":
                            product(bank, w[i], hbuf).then_inc(proj[x], 1)
                        else:
                            for t in range(B):
                                for k in range(KC):
                                    last = mm(ps[:, bank, t * P:(t + 1) * P], hbuf[:, k, t * P:(t + 1) * P],
                                              w[i][:, k, :], start=(k == 0), stop=(k == KC - 1))
                            last.then_inc(proj[x], 1)

                    def rotate(x, i):
                        pe.wait_ge(copied[x], hg + 1)
                        if x == "k":
                            pe.wait_ge(roped["q"], hg + 1)
                        else:
                            after(pe, roped["k"], hg)
                        mm(ps[:, 2, 0:S], rot, qkraw[:, i, 0:S], start=True, stop=True).then_inc(rotated[x], 1)

                    if do_att:
                        scores(0)
                    if do_proj:
                        project("q", 0, 0, copied["v"], hg)
                    if do_att:
                        turn(0)
                        scores(1)
                    if do_proj:
                        rotate("q", 0)
                        project("k", 1, 1, o_copied, hg - 1)
                    if do_att:
                        turn(1)
                        if B > 2:
                            scores(2)
                    if do_proj:
                        rotate("k", 1)
                        project("v", 2, 0, copied["q"], hg + 1)
                    if do_att:
                        for j in range(2, B):
                            turn(j)
                            if j + 1 < B:
                                scores(j + 1)
                        pe.wait_ge(turned_copied, q0 + B)
                        pe.wait_ge(copied["v"], hg)
                        if do_proj:
                            pe.wait_ge(copied["k"], hg + 1)
                        for kb in range(B):
                            last = mm(ps[:, 1, 0:S], vh[:, 1 - par_, kb * P:(kb + 1) * P],
                                      amix_t[:, kb, 0:S], start=(kb == 0), stop=(kb == B - 1))
                        last.then_inc(pv_done, 1)

                head(0, 0, True, False)
                head(1, 1, True, True)
                with pe.Fori(0, HEADS // 2 - 1) as i:
                    head(2 * i + 2, 0, True, True)
                    head(2 * i + 3, 1, True, True)
                head(HEADS, 0, False, True)

                for h in range(HEADS):
                    pe.wait_ge(sq_ready, nsq + 8 + h + 1)
                    pe.wait_ge(var_ready, 10 * g + 1 + h)
                    mm(ps[:, 2, 0:S], ones, sq[:, h % 2, 0:S], start=True, stop=True).then_inc(sq_summed, 1)
                for c in range(4):
                    n = 4 * g + c
                    pe.wait_ge(pool_diff, n + 1)
                    if c < 2:
                        pe.wait_ge(o_copied, 8 * (g + 1))
                    else:
                        pe.wait_ge(mix_copied, n - 1)
                    mm(ps[:, c % 2, 0:S], poolw[:, c, :], pdif[:, c, 0:S], start=True,
                       stop=True).then_inc(mix_done, 1)
                pe.wait_ge(mix_copied, 4 * g + 4)
                pe.wait_ge(o_normed, 8 * g + 8)

                def chunk(c, j):
                    u = b + 9 + j
                    pe.wait_ge(unit_in[u % 2], 16 * (u // 2 + 1) + 8 * (c - j))
                    after(pe, z_ready, c + (8 * g - 1) if not isinstance(c, int) else (8 * g + c - 1) * (c > 1))
                    product(4 * j, wtile(u, 0), hbuf)
                    product(4 * j + 1, wtile(u, 1), hbuf)
                    product(4 * j + 2, wtile(u, 2), obuf)
                    product(4 * j + 3, wtile(u, 3), pdif, 4).then_inc(z_done, 1)

                chunk(0, 0)
                chunk(1, 1)
                with pe.Fori(1, KC // 2) as i:
                    for j in range(2):
                        chunk(2 * i + j, j)
                pe.wait_ge(z_ready, 8 * g + 8)

                for c in range(KC):
                    u = b + 17 + c // 4
                    if c % 4 == 0:
                        unit_landed(pe, u)
                    if c >= 2:
                        pe.wait_ge(x1_ready, 8 * g + c - 1)
                    product(c % 2, wtile(u, c % 4), zbuf).then_inc(out_done, 1)
                pe.wait_ge(x1_ready, 8 * g + 8)
                for t in range(B):
                    after(pe, x1_copied, tbase[g] + t)
                    for k in range(KC):
                        last = nc.tensor.transpose(ps[:, 6 + k // 4, (k % 4) * P:(k % 4 + 1) * P],
                                                   hbuf[:, k, t * P:(t + 1) * P], ident)
                    last.then_inc(x1_turned, 1)
                sum_squares(nsq + 16)
                pe.wait_ge(norm_done, 2 * g + 2)

                pe.wait_ge(keys_in, 16 * (g + 1))

                def key_scores(h):
                    n = 8 * g + h
                    pe.wait_ge(pq_copied, n + 1)
                    if h >= 2:
                        pe.wait_ge(keyed_copied, n - 1)
                    for t in range(B):
                        bank = 2 + 2 * (h % 2) + t // 2
                        o = (t % 2) * 2 * P
                        last = mm(ps[:, bank, o:o + 2 * P], qh[:, h % 2, t * P:(t + 1) * P], keybd[:, h, :],
                                  start=True, stop=True)
                    last.then_inc(keyed, 1)

                for h in range(HEADS):
                    u = b + 19 + h // 4
                    if h % 4 == 0:
                        unit_landed(pe, u)
                    if h >= 2:
                        pe.wait_ge(pq_copied, 8 * g + h - 1)
                    product(h % 2, wtile(u, h % 4), h2).then_inc(pq_done, 1)
                    if h:
                        key_scores(h - 1)
                key_scores(HEADS - 1)

                pe.wait_ge(sel_ready, g + 1)
                for t in range(B):
                    n = tbase[g] + t
                    if t >= 2:
                        pe.wait_ge(sel_copied, n - 1)
                    elif t == 0:
                        pe.wait_ge(pq_copied, 8 * g + 8)
                    for x in range(3):
                        last = nc.tensor.transpose(ps[:, t % 2, x * P:(x + 1) * P], sel[:, t, x, :], ident)
                    last.then_inc(sel_turned, 1)
                pe.wait_ge(sel_copied, tbase[g] + B)
                all_done(pe)

                for n in range(passes[g]):
                    pp = pbase[g] + n
                    if n:
                        all_done(pe)
                    s0 = pp * (TOK // 4)

                    def gate_step(s, j):
                        pe.wait_ge(hot_ready, s + 1)
                        after(pe, g_copied, s - 1)
                        for t in range(4):
                            last = mm(ps[:, j, t * P:(t + 1) * P], onehot[:, j, 0, t, :],
                                      onehot[:, j, 1, t, :], start=True, stop=True)
                        last.then_inc(g_done, 1)

                    gate_step(s0, 0)
                    gate_step(s0 + 1, 1)
                    with pe.Fori(1, TOK // 8) as i:
                        for j in range(2):
                            gate_step(2 * i + (s0 + j), j)
                    pe.wait_ge(g_copied, s0 + TOK // 4)

                    def score(t, waits):
                        for s_, n_ in waits:
                            pe.wait_ge(s_, n_)
                        ut, _ = exp_tile(t)
                        for k in range(KC):
                            last = mm(ps[:, t % 2, 0:TOK], ut[:, k, :], h2[:, k, n * TOK:(n + 1) * TOK],
                                      start=(k == 0), stop=(k == KC - 1))
                        last.then_inc(s_done, 1)

                    def combine(t, ready, start=False, stop=False):
                        pe.wait_ge(coef_ready, ready)
                        _, v = exp_tile(t)
                        for tb in range(2):
                            for f in range(2):
                                last = mm(ps[:, 4 + 2 * tb + f, :], coef[:, t % 2, tb * P:(tb + 1) * P],
                                          v[:, f * 512:(f + 1) * 512], start=start, stop=stop,
                                          skip_group_check=True)
                        last.then_inc(v_done, 1)

                    def landed(e, t):
                        return tile_in[t], 4 * (e - t) + (16 * pp * (P // 4) + 16)

                    c0 = pp * P
                    score(0, [landed(0, 0)])
                    score(1, [landed(1, 1)])
                    combine(0, c0 + 1, start=True)
                    score(2, [landed(2, 2), (gelu_done, c0 + 1)])
                    combine(1, c0 + 2)
                    with pe.Fori(0, P // 4 - 1) as i:
                        for t in range(4):
                            e = 4 * i + (3 + t)
                            slot = (3 + t) % 4
                            score(slot, [landed(e, slot), (gelu_done, e + (c0 - 1))])
                            combine((slot + 3) % 4, e + c0)
                    score(3, [landed(P - 1, 3), (gelu_done, c0 + P - 2)])
                    combine(2, c0 + P - 1)
                    combine(3, c0 + P, stop=True)

                    for k in range(KC):
                        pe.wait_ge(diag_ready, pp * KC + k + 1)
                        mm(ps[:, 2 + k // 4, (k % 4) * P:(k % 4 + 1) * P], ones, f_diag[:, k % 2, :],
                           start=True, stop=True).then_inc(gt2_done, 1)

        @block.scalar
        def _(act):
            A = nc.scalar.activation
            act.wait_ge(consts_in, 32)
            cs = par[:, V_C:V_C + 16].rearrange("p (k g) -> p k g", g=2)
            A(silu_c[:], cs, ACT.Sigmoid).then_inc(silu_a, 1)
            act.wait_ge(lam_dot, 1)
            A(small[:, 2:4], small[:, 0:2], ACT.Exp).then_inc(lam_exp, 1)

            for g, S in enumerate(SEQS):
                B = S // P
                if g:
                    all_done(act)
                nsq = g * 24

                def squares(n0):
                    for c in range(KC):
                        if c >= 2:
                            act.wait_ge(sq_summed, n0 + c - 1)
                        A(sq[:, c % 2, 0:S], hbuf[:, c, 0:S], ACT.Square).then_inc(sq_ready, 1)

                act.wait_ge(group_in, 48 * (g + 1))
                squares(nsq)
                act.wait_ge(var_ready, 10 * g + 1)
                A(rstd[:, 0:S], rstd[:, 0:S], ACT.Sqrt).then_inc(rstd_ready, 1)
                for c in range(4):
                    act.wait_ge(p_done, 4 * g + c + 1)
                    nc.scalar.copy(pbuf[:, c, PAD:PAD + S], ps[:, c % 2, 0:S]).then_inc(p_copied, 1)

                def head(h, par_, do_proj, do_att):
                    hg = 8 * g + h
                    q0 = qbase[g] + (h - 1) * B

                    def expo(j):
                        pe_ = j % 2
                        act.wait_ge(maxed, q0 + j + 1)
                        after(act, mixed, q0 + j - 1)
                        for m in range(2):
                            last = A(expd[:, pe_, m, 0:S], ps[:, 3 + m, 0:S], ACT.Exp,
                                     bias=small[:, 4 + 2 * pe_ + m:5 + 2 * pe_ + m], scale=HALF ** -0.5,
                                     accum_out=small[:, 8 + 2 * pe_ + m:9 + 2 * pe_ + m])
                        last.then_inc(expd_ready, 1)

                    def turned_out(j):
                        act.wait_ge(turned, q0 + j + 1)
                        if j == 0:
                            after(act, pv_done, hg - 1)
                        nc.scalar.copy(amix_t[:, 0:B, j * P:(j + 1) * P],
                                       ps[:, 5, 0:S].rearrange("p (b n) -> p b n", n=P)).then_inc(turned_copied, 1)

                    def raw_out(x, i, bank):
                        act.wait_ge(proj[x], hg + 1)
                        if x == "v":
                            after(act, pv_done, hg - 1)
                            nc.scalar.copy(vh[:, par_, 0:S], ps[:, bank, 0:S]).then_inc(copied[x], 1)
                        else:
                            after(act, roped[x], hg)
                            nc.scalar.copy(qkraw[:, i, 0:S], ps[:, bank, 0:S]).then_inc(copied[x], 1)

                    if do_att:
                        expo(0)
                    if do_proj:
                        raw_out("q", 0, 0)
                    if do_att:
                        turned_out(0)
                        expo(1)
                    if do_proj:
                        raw_out("k", 1, 1)
                    if do_att:
                        turned_out(1)
                        if B > 2:
                            expo(2)
                    if do_proj:
                        raw_out("v", 2, 0)
                    if do_att:
                        for j in range(2, B):
                            turned_out(j)
                            if j + 1 < B:
                                expo(j + 1)
                        act.wait_ge(pv_done, hg)
                        hh = h - 1
                        dst = (obuf[:, hh, 0:S] if isinstance(hh, int)
                               else obuf[:, bass.ds(hh, 1), 0:S].rearrange("p a s -> p (a s)"))
                        nc.scalar.copy(dst, ps[:, 1, 0:S]).then_inc(o_copied, 1)

                head(0, 0, True, False)
                head(1, 1, True, True)
                with act.Fori(0, HEADS // 2 - 1) as i:
                    head(2 * i + 2, 0, True, True)
                    head(2 * i + 3, 1, True, True)
                head(HEADS, 0, False, True)
                act.drain()
                for h in range(HEADS):
                    if h >= 2:
                        act.wait_ge(sq_summed, nsq + 8 + h - 1)
                    A(sq[:, h % 2, 0:S], obuf[:, h, 0:S], ACT.Square).then_inc(sq_ready, 1)
                    if h:
                        act.wait_ge(var_ready, 10 * g + 1 + h)
                        A(orstd[(h - 1) % 2][:, 0:S], orstd[(h - 1) % 2][:, 0:S], ACT.Sqrt).then_inc(rstd_ready, 1)
                act.wait_ge(var_ready, 10 * g + 1 + HEADS)
                A(orstd[1][:, 0:S], orstd[1][:, 0:S], ACT.Sqrt).then_inc(rstd_ready, 1)
                for c in range(4):
                    act.wait_ge(mix_done, 4 * g + c + 1)
                    A(pdif[:, c, 0:S], ps[:, c % 2, 0:S], ACT.Copy,
                      scale=par[:, V_PSC + c:V_PSC + c + 1]).then_inc(mix_copied, 1)
                for c in range(KC):
                    act.wait_ge(z_done, 8 * g + c + 1)
                    if c >= 2:
                        act.wait_ge(z_ready, 8 * g + c - 1)
                    for m in range(2):
                        last = A(expd[:, c % 2, m, 0:S], ps[:, 4 * (c % 2) + m, 0:S], ACT.Sigmoid,
                                 bias=par[:, V_BGATE + 8 * m + c:V_BGATE + 8 * m + c + 1])
                    last.then_inc(sig_done, 1)
                for t in range(B):
                    act.wait_ge(x1_turned, tbase[g] + t + 1)
                    if t >= 2:
                        act.wait_ge(x1_stored[t % 2], 16 * ((tbase[g] + t) // 2))
                    if t == 0:
                        act.wait_ge(x1_ready, 8 * g + 8)
                    nc.scalar.copy(x1tok[:, t % 2, :].rearrange("p (a n) -> p a n", a=2),
                                   ps[:, 6:8, :]).then_inc(x1_copied, 1)
                squares(nsq + 16)
                act.wait_ge(var_ready, 10 * g + 10)
                A(rstd[:, 0:S], rstd[:, 0:S], ACT.Sqrt).then_inc(rstd_ready, 1)
                for h in range(HEADS + 1):
                    if h < HEADS:
                        act.wait_ge(pq_done, 8 * g + h + 1)
                        if h >= 2:
                            act.wait_ge(keyed, 8 * g + h - 1)
                        nc.scalar.copy(qh[:, h % 2, 0:S], ps[:, h % 2, 0:S]).then_inc(pq_copied, 1)
                    if h:
                        m = h - 1
                        act.wait_ge(keyed, 8 * g + h)
                        if m >= 2:
                            act.wait_ge(searched, 8 * g + m - 1)
                        bank = 2 + 2 * (m % 2)
                        nc.scalar.copy(sc[:, m % 2, 0:2 * S].rearrange("p (a n) -> p a n", n=512),
                                       ps[:, bank:bank + S // 256, :]).then_inc(keyed_copied, 1)
                act.wait_ge(shifted, g + 1)
                A(sel[:, 0:B, 2, :], sel[:, 0:B, 2, :], ACT.Exp).then_inc(exped, 1)
                for t in range(B):
                    act.wait_ge(sel_turned, tbase[g] + t + 1)
                    nc.scalar.copy(sel_t[:, :, t * P:(t + 1) * P],
                                   ps[:, t % 2, 0:3 * P].rearrange("p (x n) -> p x n", n=P)).then_inc(sel_copied, 1)
                all_done(act)
                for n in range(passes[g]):
                    pp = pbase[g] + n
                    if n:
                        all_done(act)
                    with act.Fori(0, TOK // 8) as i:
                        for j in range(2):
                            act.wait_ge(g_done, 2 * i + (pp * (TOK // 4) + j + 1))
                            nc.scalar.copy(gates[:, :, bass.ds(8 * i + 4 * j, 4)],
                                           ps[:, j, :].rearrange("p (t k) -> p k t", t=4)).then_inc(g_copied, 1)
                    c0 = pp * P

                    def gelu(e, j):
                        act.wait_ge(s_done, e + (c0 + 1))
                        after(act, coef_ready, e + (c0 - 1))
                        A(gel[:, j, :], ps[:, j, 0:TOK], ACT.Gelu).then_inc(gelu_done, 1)

                    gelu(0, 0)
                    gelu(1, 1)
                    with act.Fori(0, P // 2 - 1) as i:
                        for j in range(2):
                            gelu(2 * i + (j + 2), j)
                    act.wait_ge(gt2_done, KC * (pp + 1))
                    nc.scalar.copy(f_gt2.rearrange("p (a n) -> p a n", a=2), ps[:, 2:4, :]).then_inc(gt2_copied, 1)
                    for j in range(2):
                        m = 2 * pp + j
                        act.wait_ge(y_ready, m + 1)
                        A(f_sq, f_y[:, j, :], ACT.Square, accum_out=small[:, 12:13]).then_inc(y_squared, 1)
                        act.wait_ge(y_var, m + 1)
                        A(small[:, 13:14], small[:, 13:14], ACT.Sqrt).then_inc(y_rstd, 1)

        @block.vector
        def _(dve):
            V = nc.vector
            tt, ts, stt = V.tensor_tensor, V.tensor_scalar, V.scalar_tensor_tensor
            dve.wait_ge(consts_in, 32)
            cs = par[:, V_C:V_C + 16].rearrange("p (k g) -> p k g", g=2)
            lamv = par[:, V_LAM:V_LAM + 256].rearrange("p (m k n) -> p m k n", m=2, k=2)
            tt(rtmp[:, 0:128].rearrange("p (m n) -> p m n", m=2), lamv[:, :, 0, :], lamv[:, :, 1, :], ALU.mult)
            dve.drain()
            V.tensor_reduce(small[:, 0:2], rtmp[:, 0:128].rearrange("p (m n) -> p m n", m=2), AX.X,
                            ALU.add).then_inc(lam_dot, 1)
            dve.wait_ge(silu_a, 1)
            tt(silu_c[:], silu_c[:], cs, ALU.mult).then_inc(silu_b, 1)
            dve.wait_ge(lam_exp, 1)
            stt(out=nlam[:], in0=small[:, 3:4], scalar=-LAM_INIT, in1=small[:, 2:3], op0=ALU.add, op1=ALU.subtract)
            ts(gsub[:], par[:, V_GSUB:V_GSUB + 1], 1.0 - LAM_INIT, None, ALU.mult)
            dve.wait_ge(ada_done, UNITS_ADA)
            tt(mod[:], ps[:, 0, 0:96].rearrange("p (c g) -> p c g", g=2),
               par[:, V_BADA:V_BADA + 48].unsqueeze(2).broadcast_to((P, 48, 2)), ALU.add)
            dve.drain()
            for g in range(2):
                for n, v in enumerate((V_G1, V_G2)):
                    stt(out=scl[:, g, n, :], in0=mod[:, 24 * n + 8:24 * n + 16, g], scalar=1.0,
                        in1=par[:, v:v + 8], op0=ALU.add, op1=ALU.mult)

            for g, S in enumerate(SEQS):
                B = S // P
                nsq = g * 24
                if g:
                    all_done(dve)

                def inverse(dst, src, n):
                    ts(dst, src, 1.0 / n, EPS, ALU.mult, ALU.add)
                    dve.drain()
                    return V.reciprocal(dst, dst)

                def norm(n, dst):
                    dve.wait_ge(sq_summed, nsq + 16 * n + 8)
                    inverse(rstd[:, 0:S], ps[:, 2, 0:S], D).then_inc(var_ready, 1)
                    dve.wait_ge(rstd_ready, 10 * g + 9 * n + 1)
                    for c in range(KC):
                        tt(dst[:, c, 0:S], hbuf[:, c, 0:S], rstd[:, 0:S], ALU.mult)
                    dve.drain()
                    for c in range(KC):
                        last = ts(dst[:, c, 0:S], dst[:, c, 0:S], scl[:, g, n, c:c + 1],
                                  mod[:, 24 * n + c, g:g + 1], ALU.mult, ALU.add)
                    last.then_inc(norm_done, 1)

                norm(0, hbuf)

                def head(h, par_, do_proj, do_att):
                    hg = 8 * g + h
                    q0 = qbase[g] + (h - 1) * B

                    def maxima(j):
                        pe_ = j % 2
                        nm = small[:, 4 + 2 * pe_:6 + 2 * pe_]
                        dve.wait_ge(scored, q0 + j + 1)
                        V.tensor_reduce(nm, ps[:, 3:5, 0:S], AX.X, ALU.max)
                        dve.drain()
                        ts(nm, nm, -HALF ** -0.5, None, ALU.mult).then_inc(maxed, 1)

                    def mix(j):
                        pe_ = j % 2
                        zs = small[:, 8 + 2 * pe_:10 + 2 * pe_]
                        dve.wait_ge(expd_ready, q0 + j + 1)
                        after(dve, turned, q0 + j - 1)
                        V.reciprocal(zs, zs)
                        dve.drain()
                        ts(expd[:, pe_, 1, 0:S], expd[:, pe_, 1, 0:S], zs[:, 1:2], nlam[:, 0:1], ALU.mult, ALU.mult)
                        dve.drain()
                        stt(out=amix[:, pe_, 0:S], in0=expd[:, pe_, 0, 0:S], scalar=zs[:, 0:1],
                            in1=expd[:, pe_, 1, 0:S], op0=ALU.mult, op1=ALU.add).then_inc(mixed, 1)

                    def rope_(x, i):
                        dst = qk[:, par_, i, 0:S]
                        dve.wait_ge(copied[x], hg + 1)
                        after(dve, scored, q0)
                        tt(dst, qkraw[:, i, 0:S], cossin[:, 0, 0:S], ALU.mult)
                        dve.wait_ge(rotated[x], hg + 1)
                        tt(rtmp[:, 0:S], ps[:, 2, 0:S], cossin[:, 1, 0:S], ALU.mult)
                        dve.drain()
                        tt(dst, dst, rtmp[:, 0:S], ALU.add).then_inc(roped[x], 1)

                    if do_att:
                        maxima(0)
                        mix(0)
                        maxima(1)
                    if do_proj:
                        rope_("q", 0)
                    if do_att:
                        mix(1)
                        if B > 2:
                            maxima(2)
                    if do_proj:
                        rope_("k", 1)
                    if do_att:
                        for j in range(2, B):
                            mix(j)
                            if j + 1 < B:
                                maxima(j + 1)

                head(0, 0, True, False)
                head(1, 1, True, True)
                with dve.Fori(0, HEADS // 2 - 1) as i:
                    head(2 * i + 2, 0, True, True)
                    head(2 * i + 3, 1, True, True)
                head(HEADS, 0, False, True)

                dve.drain()
                for h in range(HEADS):
                    dve.wait_ge(sq_summed, nsq + 8 + h + 1)
                    inverse(orstd[h % 2][:, 0:S], ps[:, 2, 0:S], P).then_inc(var_ready, 1)
                    dve.wait_ge(rstd_ready, 10 * g + 2 + h)
                    stt(out=obuf[:, h, 0:S], in0=obuf[:, h, 0:S], scalar=gsub[:, 0:1], in1=orstd[h % 2][:, 0:S],
                        op0=ALU.mult, op1=ALU.mult).then_inc(o_normed, 1)
                for c in range(KC):
                    k = 4 * (c % 2)
                    dve.wait_ge(sig_done, 8 * g + c + 1)
                    tt(zbuf[:, c, 0:S], ps[:, k + 3, 0:S], expd[:, c % 2, 0, 0:S], ALU.mult)
                    att = expd[:, c % 2, 1, 0:S]
                    tt(att, ps[:, k + 2, 0:S], att, ALU.mult)
                    dve.drain()
                    tt(zbuf[:, c, 0:S], zbuf[:, c, 0:S], att, ALU.add).then_inc(z_ready, 1)
                dve.wait_ge(x_again, 16 * (g + 1))
                for c in range(KC):
                    dve.wait_ge(out_done, 8 * g + c + 1)
                    stt(out=hbuf[:, c, 0:S], in0=ps[:, c % 2, 0:S], scalar=mod[:, 16 + c, g:g + 1],
                        in1=obuf[:, c, 0:S], op0=ALU.mult, op1=ALU.add).then_inc(x1_ready, 1)
                dve.drain()
                norm(1, h2)

                def top16(src, spare, val, idx):
                    V.max(val[:, 0:8], src)
                    dve.drain()
                    V.max_index(idx[:, 0:8], val[:, 0:8], src)
                    V.match_replace(spare, val[:, 0:8], src, NEG)
                    dve.drain()
                    V.max(val[:, 8:16], spare)
                    dve.drain()
                    V.max_index(idx[:, 8:16], val[:, 8:16], spare)

                iota16 = iota[:, 0:TOPK]
                flat = lambda t: t.rearrange("p a b -> p (a b)")
                for h in range(HEADS):
                    dve.wait_ge(keyed_copied, 8 * g + h + 1)
                    scores = sc[:, h % 2, 0:2 * S].rearrange("p (t x n) -> p t x n", x=2, n=P)
                    for t in range(B):
                        for x in range(2):
                            top16(scores[:, t, x, :], sc2[:, x * P:(x + 1) * P], best[:, t, x, :],
                                  besti[:, t, x, :].bitcast(U32))
                    dve.drain()
                    V.tensor_copy(bestf[:, 0:B], besti[:, 0:B].bitcast(U32))
                    for t in range(B):
                        tt(cand, best[:, t, 0, :].unsqueeze(2).broadcast_to((P, TOPK, TOPK)),
                           best[:, t, 1, :].unsqueeze(1).broadcast_to((P, TOPK, TOPK)), ALU.add)
                        dve.drain()
                        top16(flat(cand), flat(cand2), sel[:, t, 2, h * TOPK:(h + 1) * TOPK], jbest.bitcast(U32))
                        dve.drain()
                        ts(jhalf[:, 0, :].bitcast(U32), jbest.bitcast(U32), 4, None, ALU.logical_shift_right)
                        ts(jhalf[:, 1, :].bitcast(U32), jbest.bitcast(U32), TOPK - 1, None, ALU.bitwise_and)
                        dve.drain()
                        V.tensor_copy(jf, jhalf.bitcast(U32))
                        dve.drain()
                        for x in range(2):
                            tt(mask[:, x], jf[:, x, :].unsqueeze(2).broadcast_to((P, TOPK, TOPK)),
                               iota16.unsqueeze(1).broadcast_to((P, TOPK, TOPK)), ALU.is_equal)
                        dve.drain()
                        for x in range(2):
                            tt(mask[:, x], mask[:, x], bestf[:, t, x, :].unsqueeze(1).broadcast_to((P, TOPK, TOPK)),
                               ALU.mult)
                        dve.drain()
                        for x in range(2):
                            last = V.tensor_reduce(sel[:, t, x, h * TOPK:(h + 1) * TOPK], mask[:, x], AX.X, ALU.add)
                    last.then_inc(searched, 1)
                dve.drain()
                for t in range(B):
                    v = sel[:, t, 2, :].rearrange("p (h k) -> p h k", k=TOPK)
                    V.tensor_copy(gsum[:, 0:HEADS], v[:, :, 0])
                    dve.drain()
                    tt(v, v, gsum[:, 0:HEADS].unsqueeze(2).broadcast_to((P, HEADS, TOPK)), ALU.subtract)
                    dve.drain()
                V.tensor_copy(gsum[:, 0:1], gsum[:, 0:1]).then_inc(shifted, 1)
                dve.wait_ge(exped, g + 1)
                for t in range(B):
                    v = sel[:, t, 2, :].rearrange("p (h k) -> p h k", k=TOPK)
                    V.tensor_reduce(gsum[:, 0:HEADS], v, AX.X, ALU.add)
                    dve.drain()
                    V.reciprocal(gsum[:, 0:HEADS], gsum[:, 0:HEADS])
                    dve.drain()
                    tt(v, v, gsum[:, 0:HEADS].unsqueeze(2).broadcast_to((P, HEADS, TOPK)), ALU.mult)
                    dve.drain()
                V.tensor_copy(gsum[:, 0:1], gsum[:, 0:1]).then_inc(sel_ready, 1)
                all_done(dve)

                for n in range(passes[g]):
                    pp = pbase[g] + n
                    if n:
                        all_done(dve)
                    s0 = pp * (TOK // 4)

                    def hot_step(s, tok, j):
                        after(dve, g_done, s - 1)
                        for t in range(4):
                            col = bass.ds(tok + t, 1) if not isinstance(tok, int) else slice(tok + t, tok + t + 1)
                            ts(onehot[:, j, 0, t, :], iota, sel_t[:, 0, col], None, ALU.is_equal)
                            last = ts(onehot[:, j, 1, t, :], iota, sel_t[:, 1, col], sel_t[:, 2, col],
                                      ALU.is_equal, ALU.mult)
                        last.then_inc(hot_ready, 1)

                    hot_step(s0, n * TOK, 0)
                    hot_step(s0 + 1, n * TOK + 4, 1)
                    with dve.Fori(1, TOK // 8) as i:
                        for j in range(2):
                            hot_step(2 * i + (s0 + j), 8 * i + (n * TOK + 4 * j), j)
                    dve.wait_ge(g_copied, s0 + TOK // 4)

                    c0 = pp * P

                    def coefficient(e, j):
                        dve.wait_ge(gelu_done, e + (c0 + 1))
                        after(dve, v_done, e + (c0 - 1))
                        w = gates[:, e, :] if isinstance(e, int) else \
                            gates[:, bass.ds(e, 1), :].rearrange("p a t -> p (a t)")
                        tt(coef[:, j, :], gel[:, j, :], w, ALU.mult).then_inc(coef_ready, 1)

                    coefficient(0, 0)
                    coefficient(1, 1)
                    with dve.Fori(0, P // 2 - 1) as i:
                        for j in range(2):
                            coefficient(2 * i + (j + 2), j)

                    dve.drain()
                    for k in range(KC):
                        if k >= 2:
                            dve.wait_ge(gt2_done, pp * KC + k - 1)
                        ts(f_diag[:, k % 2, :], ident, mod[:, 40 + k, g:g + 1], None, ALU.mult).then_inc(diag_ready, 1)
                    dve.wait_ge(gt2_copied, pp + 1)
                    dve.wait_ge(v_done, (pp + 1) * P)
                    dve.wait_ge(fin_in, 48 * (pp + 1))
                    for j in range(2):
                        m = 2 * pp + j
                        y = f_y[:, j, :]
                        tt(y.rearrange("p (a n) -> p a n", a=2), ps[:, 4 + 2 * j:6 + 2 * j, :],
                           f_gt2.rearrange("p (a n) -> p a n", a=2), ALU.mult)
                        dve.drain()
                        tt(y, y, f_x1[:, j, :], ALU.add).then_inc(y_ready, 1)
                        dve.wait_ge(y_squared, m + 1)
                        inverse(small[:, 13:14], small[:, 12:13], D).then_inc(y_var, 1)
                        dve.wait_ge(y_rstd, m + 1)
                        stt(out=y, in0=y, scalar=small[:, 13:14], in1=f_gf, op0=ALU.mult,
                            op1=ALU.mult).then_inc(y_final, 1)

        @block.gpsimd
        def _(pool):
            G = nc.gpsimd
            for g, S in enumerate(SEQS):
                if g:
                    all_done(pool)
                L = S + 2 * PAD
                G.memset(pbuf[:, :, 0:PAD], 0.0)
                G.memset(pbuf[:, :, PAD + S:L], 0.0)
                for c, w in enumerate(WINDOWS):
                    pool.wait_ge(p_copied, 4 * g + c + 1)
                    src, lo = pbuf[:, c, :], 0
                    for n in range(c + 1):
                        d = max(1, 2 ** n // 2)
                        dst = ptmp[:, n % 2, :]
                        lo, back, ahead = (1, 1, 0) if n == 0 else (lo + d, d, d)
                        pool.drain()
                        G.tensor_tensor(dst[:, lo:L - lo], src[:, lo - back:L - lo - back],
                                        src[:, lo + ahead:L - lo + ahead], ALU.add)
                        src = dst
                    pool.drain()
                    mean = src[:, PAD:PAD + S]
                    G.tensor_scalar(mean, mean, 1.0 / w, None, ALU.mult)
                    pool.drain()
                    G.tensor_tensor(mean[:, 0:PAD], mean[:, 0:PAD], edge[:, c, 0:PAD], ALU.mult)
                    G.tensor_tensor(mean[:, S - PAD:S], mean[:, S - PAD:S], edge[:, c, PAD:2 * PAD], ALU.mult)
                    pool.drain()
                    G.tensor_tensor(pdif[:, c, 0:S], mean, pbuf[:, c, PAD:PAD + S], ALU.subtract).then_inc(pool_diff, 1)
                all_done(pool)
                for n in range(1, passes[g]):
                    all_done(pool)


def shape_constants():
    c = np.zeros((P, C_N), np.float32)
    c[:, C_ID:C_ID + P] = np.eye(P)
    c[:, C_ONE:C_ONE + P] = 1
    for i in range(P):
        if i % HALF < HALF // 2:
            c[i + HALF // 2, C_ROT + i] = -1
        else:
            c[i - HALF // 2, C_ROT + i] = 1
    c[:, C_IOTA:C_IOTA + P] = np.arange(P)
    for n, w in enumerate(WINDOWS):
        for i in range(PAD):
            c[:, C_EDGE + 16 * n + i] = w / (min(i + w // 2, SMAX) - max(i - w // 2, 0))
            back = PAD - i
            c[:, C_EDGE + 16 * n + PAD + i] = w / (min(w // 2, back) + w // 2)
    inv = (1.0 / (10000.0 ** (np.arange(0, HALF, 2, dtype=np.float32) / HALF))).astype(np.float32)
    ang = np.arange(SMAX, dtype=np.float32)[None, :] * np.tile(inv, 4)[:, None]
    rope = np.stack([np.cos(ang), np.sin(ang)], axis=1).astype(np.float32)
    return c, rope


def kernel(**inputs):
    import concourse.bacc as _bacc
    from concourse.bass_utils import run_bass_kernel_spmd as _run

    a = {k: np.asarray(v) for k, v in inputs.items()}
    f = np.float32

    def tiles(w):
        r, n = w.shape
        return w.reshape(r // P, P, n // P, P).transpose(2, 1, 0, 3)

    units = np.zeros((UNITS_ADA + UNITS_GROUP, P, 4, KC, P), f)
    units[:UNITS_ADA] = tiles(a["w_ada"][0]).reshape(UNITS_ADA, 4, P, KC, P).transpose(0, 2, 1, 3, 4)
    u = units[UNITS_ADA:]
    w_in = tiles(a["w_in"][0])
    gate, att, out_, peer = (tiles(a[k][0]) for k in ("w_gate", "w_att_out", "w_out", "w_peer_q"))
    po = tiles(a["w_pool_out"][0])
    for i in range(4):
        u[0][:, i] = w_in[i]
    for h in range(HEADS):
        for i in range(3):
            u[1 + h][:, i] = w_in[4 + 8 * i + h]
    for c in range(KC):
        u[9 + c][:, 0], u[9 + c][:, 1], u[9 + c][:, 2] = gate[c], gate[KC + c], att[c]
        u[9 + c][:, 3, 0:4] = po[c]
        u[17 + c // 4][:, c % 4] = out_[c]
        u[19 + c // 4][:, c % 4] = peer[c]

    def cols(v):
        return v.reshape(-1, P).T

    params = np.zeros((P, V_N), f)
    for at, v in ((V_G1, a["g_norm1"]), (V_G2, a["g_norm2"]), (V_BADA, a["b_ada"]), (V_BGATE, a["b_gate"]),
                  (V_PSC, a["pool_scale"]), (V_GSUB, a["g_sub"])):
        c = cols(v[0])
        params[:, at:at + c.shape[1]] = c
    cc = np.stack([a["c_prompt"][0].reshape(KC, P), a["c_sample"][0].reshape(KC, P)], axis=2)
    params[:, V_C:V_C + 16] = cc.transpose(1, 0, 2).reshape(P, 16)
    params[:, V_LAM:] = np.concatenate([a[k][0] for k in ("lam_q1", "lam_k1", "lam_q2", "lam_k2")])[None, :]
    keys = np.zeros((P, HEADS, 2 * P), f)
    for x in range(2):
        keys[HALF * x:HALF * (x + 1), :, P * x:P * (x + 1)] = a["peer_keys"][0][:, x].transpose(2, 0, 1)
    consts, rope = shape_constants()
    x_t = [a[k][0].T.reshape(KC, P, -1).transpose(1, 0, 2) for k in ("x_prompt", "x_sample")]
    eu = a["peer_u"][0].reshape(P, P, KC, P).transpose(1, 3, 2, 0).reshape(P, P, D)
    ev = a["peer_v"][0].reshape(P, P, D).transpose(1, 0, 2)
    sent = {
        "consts": consts, "params": params, "rope": rope, "keys": keys,
        "pool_w": a["pool_w"][0].transpose(1, 0, 2), "g_final": np.broadcast_to(a["g_final"], (P, D)),
        "x_t0": x_t[0], "x_t1": x_t[1], "weights": units.reshape(-1, P, UNIT),
        "table": np.concatenate([eu, ev], axis=2),
    }
    sent = {"in_" + k: np.ascontiguousarray(v) for k, v in sent.items()}
    nc = _bacc.Bacc("TRN2", target_bir_lowering=False, num_devices=1)
    ap = {k: nc.dram_tensor(k, v.shape, mybir.dt.from_np(v.dtype), kind="ExternalInput").ap() for k, v in sent.items()}
    outs = [nc.dram_tensor("out_%d" % g, (1, S, D), F32, kind="ExternalOutput").ap() for g, S in enumerate(SEQS)]
    build(nc, ap["in_consts"], ap["in_params"], ap["in_rope"], ap["in_keys"], ap["in_pool_w"], ap["in_g_final"],
          [ap["in_x_t0"], ap["in_x_t1"]], ap["in_weights"], ap["in_table"], outs)
    r = _run(nc, [sent], core_ids=[0])
    return tuple(r.results[0]["out_%d" % g] for g in range(2))
```

```python
from contextlib import ExitStack

import numpy as np

import concourse.bass as bass
from concourse import mybir

F32 = mybir.dt.float32
F32R = mybir.dt.float32r
U32 = mybir.dt.uint32
ALU = mybir.AluOpType
ACT = mybir.ActivationFunctionType
AX = mybir.AxisListType

P = 128
D = 1024
KC = D // P
HEADS = 8
HALF = 64
TOPK = 16
SEQS = (256, 512)
SMAX = max(SEQS)
EPS = 1e-6
LAM_INIT = 0.2
WINDOWS = (2, 4, 8, 16)
PAD = 8
LROW = SMAX + 2 * PAD
TOK = 256
PASSES = sum(SEQS) // TOK
STAGE = 64
TILE = KC * P
UNIT = 4 * TILE
UNITS_ADA = 12
UNITS_GROUP = 21
NEG = -3.0e38

C_ID, C_ONE, C_ROT, C_IOTA, C_EDGE, C_N = 0, 128, 256, 384, 512, 512 + 4 * 16
V_G1, V_G2, V_BADA, V_BGATE, V_PSC, V_GSUB, V_C, V_LAM, V_N = 0, 8, 16, 64, 80, 84, 85, 101, 101 + 4 * 64


def after(eng, sem, n):
    if isinstance(n, int) and n <= 0:
        return
    eng.wait_ge(sem, n)


def build(nc, consts, params, rope, keys, pool_w, g_final, x_t, weights, table, outs):
    with ExitStack() as ctx:
        def sb(name, shape, dt=F32):
            return ctx.enter_context(nc.sbuf_tensor(name, shape, dt))

        def sem(name):
            return ctx.enter_context(nc.semaphore(name))

        def scratch(name, *shape):
            return nc.dram_tensor(name, shape, F32, kind="Internal").ap()

        blocks = sum(SEQS) // P
        x1_dram = scratch("x1_scratch", blocks, P, D)
        h2_dram = scratch("h2_scratch", PASSES, P, KC, TOK)
        score_dram = scratch("score_scratch", blocks * HEADS, P, 2 * P)
        gt2_dram = scratch("gt2_scratch", 2, P, D)
        gate_dram = scratch("gate_scratch", PASSES, P, P, TOK)

        cst = sb("cst", [P, C_N])
        ident, ones, rot = cst[:, C_ID:C_ID + P], cst[:, C_ONE:C_ONE + P], cst[:, C_ROT:C_ROT + P]
        iota = cst[:, C_IOTA:C_IOTA + P]
        edge = cst[:, C_EDGE:C_EDGE + 64].rearrange("p (g n) -> p g n", g=4)
        mod = sb("mod", [P, 48, 2])
        scl = sb("scl", [P, 2, 2, KC])
        silu_c = sb("silu_c", [P, KC, 2])
        small = sb("small", [P, 16])
        gsub = sb("gsub", [P, 1])
        nlam = sb("nlam", [P, 1])
        trunk_memory = ExitStack()

        def trunk_sb(name, shape, dt=F32):
            return trunk_memory.enter_context(nc.sbuf_tensor(name, shape, dt))

        ring = trunk_sb("ring", [P, 2 * UNIT])
        arena = trunk_sb("arena", [P, P * TOK])
        par = trunk_sb("par", [P, V_N])

        place = [0]

        def lay(*dims):
            n = int(np.prod(dims))
            a = arena[:, place[0]:place[0] + n]
            place[0] += n
            names = "abcd"[:len(dims)]
            if len(dims) > 1:
                a = a.rearrange("p (%s) -> p %s" % (" ".join(names), " ".join(names)),
                                **{k: v for k, v in zip(names, dims)})
            return a

        hbuf = lay(KC, SMAX)
        obuf = lay(KC, SMAX)
        zbuf = lay(KC, SMAX)
        pbuf = lay(4, LROW)
        ptmp = lay(2, LROW)
        pdif = lay(4, SMAX)
        qk = lay(2, 2, SMAX)
        qkraw = lay(2, SMAX)
        rtmp = lay(SMAX)
        vh = lay(2, SMAX)
        expd = lay(2, 2, SMAX)
        amix = lay(2, SMAX)
        amix_t = lay(4, SMAX)
        sq = lay(2, SMAX)
        rstd = lay(SMAX)
        orstd = (rstd, rtmp)
        cossin = lay(2, SMAX)
        poolw = lay(4, P)
        assert place[0] <= P * TOK, place
        base_topk = 2 * KC * SMAX
        place[0] = base_topk
        keybd = lay(HEADS, 2 * P)
        qh = lay(2, SMAX)
        place[0] = base_topk + KC * SMAX
        sc = lay(2, 4 * 2 * P)
        x1tok = lay(2, D)
        gt2row = lay(D)
        diag = lay(2, P)
        trunk_memory.close()

        raw = sb("raw", [P, 4, 2 * D])
        gate_in = sb("gate_in", [P, 4, TOK])
        u_hi, u_lo = sb("u_hi", [P, 2, KC, P], F32R), sb("u_lo", [P, 2, KC, P], F32R)
        v_hi, v_lo = sb("v_hi", [P, 2, D], F32R), sb("v_lo", [P, 2, D], F32R)
        h_hi, h_lo = sb("h_hi", [P, KC, TOK], F32R), sb("h_lo", [P, KC, TOK], F32R)
        c_hi, c_lo = sb("c_hi", [P, 2, TOK], F32R), sb("c_lo", [P, 2, TOK], F32R)
        coef = sb("coef", [P, 2, TOK])
        staged = sb("staged", [P, P, 2 * STAGE])
        hot1, hot2h, hot2l = (sb(n, [P, 2, 4, P], F32R) for n in ("hot1", "hot2h", "hot2l"))
        score_in = sb("score_in", [P, 2, P])
        spare = sb("spare", [P, 2, P])
        best, besti, bestf = sb("best", [P, 2, TOPK]), sb("besti", [P, 2, TOPK], U32), sb("bestf", [P, 2, TOPK])
        cand = sb("cand", [P, 2, TOPK, TOPK])
        pair = sb("pair", [P, TOPK])
        jbest, jhalf, jf = sb("jbest", [P, TOPK], U32), sb("jhalf", [P, 2, TOPK], U32), sb("jf", [P, 2, TOPK])
        sel = sb("sel", [P, 3, 2 * P])
        gsum = sb("gsum", [P, 16])
        sel_t = sb("sel_t", [P, 3, TOK])
        gate_hi = sb("gate_hi", [P, TOK], F32R)
        gate_lo = sb("gate_lo", [P, TOK])
        f_gt2, f_gf = sb("f_gt2", [P, D]), sb("f_gf", [P, D])
        f_x1, f_y = sb("f_x1", [P, 2, D]), sb("f_y", [P, 2, D])

        ps = ctx.enter_context(nc.psum_tensor("ps", [P, 8, 512], F32))

        consts_in = sem("consts_in")
        group_in = sem("group_in")
        phase = sem("phase")
        unit_in = [sem("unit_in0"), sem("unit_in1")]
        silu_a, silu_b, ada_done = sem("silu_a"), sem("silu_b"), sem("ada_done")
        lam_dot, lam_exp = sem("lam_dot"), sem("lam_exp")
        sq_ready, sq_summed, var_ready, rstd_ready, norm_done = (
            sem("sq_ready"), sem("sq_summed"), sem("var_ready"), sem("rstd_ready"), sem("norm_done"))
        p_done, p_copied, pool_pad, pool_diff = sem("p_done"), sem("p_copied"), sem("pool_pad"), sem("pool_diff")
        mix_done, mix_copied = sem("mix_done"), sem("mix_copied")
        proj = {k: sem(k + "_proj") for k in "qkv"}
        copied = {k: sem(k + "_copied") for k in "qkv"}
        rotated = {k: sem(k + "_rotated") for k in "qk"}
        roped = {k: sem(k + "_roped") for k in "qk"}
        scored, maxed, expd_ready, mixed, turned, turned_copied = (
            sem("scored"), sem("maxed"), sem("expd_ready"), sem("mixed"), sem("turned"), sem("turned_copied"))
        pv_done, o_copied = sem("pv_done"), sem("o_copied")
        z_done, sig_done, z_ready = sem("z_done"), sem("sig_done"), sem("z_ready")
        out_done, x1_ready, x_again = sem("out_done"), sem("x1_ready"), sem("x_again")
        x1_turned, x1_copied, x1_stored = sem("x1_turned"), sem("x1_copied"), [sem("x1_stored0"), sem("x1_stored1")]
        keys_in, pq_done, pq_copied, keyed, keyed_copied = (
            sem("keys_in"), sem("pq_done"), sem("pq_copied"), sem("keyed"), sem("keyed_copied"))
        scores_stored = [sem("scores_stored0"), sem("scores_stored1")]
        h2_stored, o_normed = sem("h2_stored"), sem("o_normed")
        diag_ready, gt2_done, gt2_copied, gt2_stored = (
            sem("diag_ready"), sem("gt2_done"), sem("gt2_copied"), sem("gt2_stored"))
        score_loaded, score_free = sem("score_loaded"), sem("score_free")
        searched, shifted, exped, sel_ready, sel_turned, sel_copied, gate_split = (
            sem("searched"), sem("shifted"), sem("exped"), sem("sel_ready"), sem("sel_turned"), sem("sel_copied"),
            sem("gate_split"))
        hot_ready, g_done, g_copied = sem("hot_ready"), sem("g_done"), sem("g_copied")
        gates_stored = [sem("gates_stored0"), sem("gates_stored1")]
        raw_in = [sem("raw_in%d" % i) for i in range(4)]
        gate_loaded = [sem("gate_loaded%d" % i) for i in range(4)]
        STEPS = TOK // 4
        h_in, h_hi_ready, h_lo_ready = sem("h_in"), sem("h_hi_ready"), sem("h_lo_ready")
        u_hi_ready, u_lo_ready, v_hi_ready, v_lo_ready = (
            sem("u_hi_ready"), sem("u_lo_ready"), sem("v_hi_ready"), sem("v_lo_ready"))
        s_done, gelu_done, coef_ready, c_hi_ready, c_lo_ready, v_done = (
            sem("s_done"), sem("gelu_done"), sem("coef_ready"), sem("c_hi_ready"), sem("c_lo_ready"), sem("v_done"))
        fin_in, acc_read, y_ready, y_squared, y_var, y_rstd, y_final, y_stored = (
            sem("fin_in"), sem("acc_read"), sem("y_ready"), sem("y_squared"), sem("y_var"), sem("y_rstd"),
            sem("y_final"), sem("y_stored"))

        block = ctx.enter_context(nc.Block())

        phases = {}

        def all_done(eng):
            n = phases[id(eng)] = phases.get(id(eng), 0) + 1
            eng.drain()
            eng.sem_inc(phase, 1)
            eng.wait_ge(phase, 5 * n)

        def wtile(u, i):
            o = (u % 2) * UNIT + i * TILE
            return ring[:, o:o + TILE].rearrange("p (k n) -> p k n", k=KC)

        def unit_landed(eng, u):
            eng.wait_ge(unit_in[u % 2], 16 * (u // 2 + 1))

        ubase = [UNITS_ADA + g * UNITS_GROUP for g in range(2)]
        qbase = [0, HEADS * SEQS[0] // P]
        group_of = (0, 1, 1)
        tbase = [0, SEQS[0] // P]

        @block.sync
        def _(sp):
            sp.dma_start(par[:], params).then_inc(consts_in, 16)
            sp.dma_start(cst[:], consts).then_inc(consts_in, 16)

            def load_unit(u, half):
                sp.dma_start(ring[:, half * UNIT:(half + 1) * UNIT], u).then_inc(unit_in[half], 16)

            def weight_unit(u):
                return weights[bass.ds(u, 1)].rearrange("a p n -> (a p) n")

            for u in range(2):
                load_unit(weights[u], u)
            with sp.Fori(1, UNITS_ADA // 2) as i:
                for j in range(2):
                    sp.wait_ge(ada_done, 2 * i + j - 1)
                    load_unit(weight_unit(2 * i + j), j)
            for g, S in enumerate(SEQS):
                if g:
                    all_done(sp)
                sp.dma_start(hbuf[:, :, 0:S], x_t[g]).then_inc(group_in, 16)
                sp.dma_start(cossin[:, :, 0:S], rope[:, :, 0:S]).then_inc(group_in, 16)
                sp.dma_start(poolw, pool_w).then_inc(group_in, 16)
                b = ubase[g]

                def load(n, used, count):
                    sp.wait_ge(used, count)
                    load_unit(weights[UNITS_ADA + n], (b + n) % 2)

                load(0, ada_done, UNITS_ADA - 1)
                load(1, ada_done, UNITS_ADA)
                load(2, p_done, 4 * g + 4)
                with sp.Fori(1, HEADS // 2) as i:
                    for j in range(2):
                        sp.wait_ge(proj["v"], 2 * i + (8 * g + j - 1))
                        load_unit(weight_unit(2 * i + (UNITS_ADA + 1 + j)), (b + 1 + j) % 2)
                load(9, proj["v"], 8 * g + 7)
                load(10, proj["v"], 8 * g + 8)
                with sp.Fori(1, KC // 2) as i:
                    for j in range(2):
                        sp.wait_ge(z_done, 2 * i + (8 * g + j - 1))
                        load_unit(weight_unit(2 * i + (UNITS_ADA + 9 + j)), (b + 9 + j) % 2)
                load(17, z_done, 8 * g + 7)
                load(18, z_done, 8 * g + 8)
                sp.wait_ge(z_done, HEADS * (g + 1))
                sp.dma_start(obuf[:, :, 0:S], x_t[g]).then_inc(x_again, 16)
                load(19, out_done, 8 * g + 4)
                load(20, out_done, 8 * g + 8)
                sp.dma_start(keybd, keys).then_inc(keys_in, 16)
                for tb in range(S // P):
                    sp.wait_ge(x1_copied, tbase[g] + tb + 1)
                    sp.dma_start(x1_dram[tbase[g] + tb], x1tok[:, tb % 2, :]).then_inc(x1_stored[tb % 2], 16)
                sp.wait_ge(norm_done, 2 * g + 2)
                for n in range(S // TOK):
                    sp.dma_start(h2_dram[g + n], obuf[:, :, n * TOK:(n + 1) * TOK]).then_inc(h2_stored, 16)
                sp.wait_ge(gt2_copied, g + 1)
                sp.dma_start(gt2_dram[g], gt2row).then_inc(gt2_stored, 16)
                for h in range(HEADS):
                    sp.wait_ge(keyed_copied, 8 * g + h + 1)
                    dst = score_dram.rearrange("(t h) p n -> h p t n", h=HEADS)[h, :, tbase[g]:tbase[g] + S // P, :]
                    sp.dma_start(dst, sc[:, h % 2, 0:2 * S].rearrange("p (t n) -> p t n", n=2 * P)
                                 ).then_inc(scores_stored[h % 2], 16)
                for j in range(2):
                    sp.wait_ge(x1_stored[j], 16 * (tbase[g] + S // P) // 2)
                    sp.wait_ge(scores_stored[j], 64 * (g + 1))
                sp.wait_ge(h2_stored, 16 * (g + S // TOK))
                sp.wait_ge(gt2_stored, 16 * (g + 1))

            all_done(sp)
            sp.dma_start(f_gf[:], g_final).then_inc(fin_in, 16)
            sp.dma_start(f_y[:].rearrange("p a n -> p (a n)"),
                         h2_dram[0].rearrange("p k t -> p (k t)")).then_inc(h_in, 16)

            def load_scores(nxt, i):
                u = i + 16 * nxt
                after(sp, score_free, u)
                src = score_dram[bass.ds(u, 1)].rearrange("a p n -> (a p) n")
                sp.dma_start(score_in[:].rearrange("p a n -> p (a n)"), src).then_inc(score_loaded, 16)

            def load_tile(n, i, t):
                k = 4 * i + (t + P * n)
                e = 4 * i + t
                after(sp, u_lo_ready, k - 3)
                after(sp, v_lo_ready, k - 3)
                sp.dma_start(raw[:, t, :], table[bass.ds(e, 1)].rearrange("a p n -> (a p) n")).then_inc(raw_in[t], 16)
                after(sp, coef_ready, k - 3)
                sp.dma_start(gate_in[:, t, :], gate_dram[n, bass.ds(e, 1)].rearrange("a p n -> (a p) n")
                             ).then_inc(gate_loaded[t], 16)

            def store_y(n):
                for j in range(2):
                    sp.wait_ge(y_final, 2 * n + j + 1)
                    r = (n - group_of[n]) * TOK + j * P
                    sp.dma_start(outs[group_of[n]][0, r:r + P, :], f_y[:, j, :]).then_inc(y_stored, 16)
                sp.wait_ge(y_stored, 32 * (n + 1))

            for n in range(-1, PASSES):
                nxt = n + 1 if n + 1 < PASSES else None

                def body(i, searching):
                    for t in range(4):
                        if searching and t == 2:
                            load_scores(nxt, i)
                        if n >= 0:
                            load_tile(n, i, t)

                if n < 0:
                    with sp.Fori(0, 16) as i:
                        body(i, True)
                    continue
                for j in range(2):
                    sp.wait_ge(gates_stored[j], 32 * (n + 1))
                body(0, nxt is not None)
                body(1, nxt is not None)
                if n:
                    store_y(n - 1)
                sp.dma_start(f_gt2[:], gt2_dram[group_of[n]]).then_inc(fin_in, 16)
                for j in range(2):
                    sp.dma_start(f_x1[:, j, :], x1_dram[2 * n + j]).then_inc(fin_in, 16)
                if nxt is not None:
                    if n == 0:
                        sp.wait_ge(h_lo_ready, 1)
                    sp.dma_start(f_y[:].rearrange("p a n -> p (a n)"),
                                 h2_dram[nxt].rearrange("p k t -> p (k t)")).then_inc(h_in, 16)
                    with sp.Fori(2, 16) as i:
                        body(i, True)
                    with sp.Fori(16, 32) as i:
                        body(i, False)
                else:
                    with sp.Fori(2, 32) as i:
                        body(i, False)
            store_y(PASSES - 1)


        @block.tensor
        def _(pe):
            mm = nc.tensor.matmul
            pe.wait_ge(consts_in, 32)
            pe.wait_ge(silu_b, 1)
            with pe.Fori(0, UNITS_ADA // 2) as u2:
                for j in range(2):
                    pe.wait_ge(unit_in[j], 16 * u2 + 16)
                    for i in range(4):
                        for k in range(KC):
                            last = mm(ps[:, 0, bass.ds(16 * u2 + (8 * j + 2 * i), 2)], wtile(j, i)[:, k, :],
                                      silu_c[:, k, :], start=(k == 0), stop=(k == KC - 1))
                    last.then_inc(ada_done, 1)

            for g, S in enumerate(SEQS):
                B = S // P
                b = ubase[g]
                if g:
                    all_done(pe)

                def sum_squares(n0):
                    for c in range(KC):
                        pe.wait_ge(sq_ready, n0 + c + 1)
                        mm(ps[:, 2, 0:S], ones, sq[:, c % 2, 0:S], start=(c == 0),
                           stop=(c == KC - 1)).then_inc(sq_summed, 1)

                def product(bank, w, src, n=KC):
                    for k in range(n):
                        last = mm(ps[:, bank, 0:S], w[:, k, :], src[:, k, 0:S], start=(k == 0), stop=(k == n - 1))
                    return last

                nsq = g * 24
                pe.wait_ge(group_in, 48 * (g + 1))
                sum_squares(nsq)
                pe.wait_ge(norm_done, 2 * g + 1)

                unit_landed(pe, b)
                for c in range(4):
                    n = 4 * g + c
                    if c >= 2:
                        pe.wait_ge(p_copied, n - 1)
                    product(c % 2, wtile(b, c), hbuf).then_inc(p_done, 1)
                pe.wait_ge(p_copied, 4 * g + 4)

                def head(h, par_, do_proj, do_att):
                    hg = 8 * g + h
                    u = b + 1 + par_
                    w = wtile(u, 0), wtile(u, 1), wtile(u, 2)
                    q0 = qbase[g] + (h - 1) * B

                    def scores(j):
                        if j == 0:
                            for x in "qk":
                                after(pe, roped[x], hg)
                        after(pe, expd_ready, q0 + j)
                        o = 1 - par_
                        for m in range(2):
                            r = slice(HALF * m, HALF * m + HALF)
                            last = mm(ps[:, 3 + m, 0:S], qk[r, o, 0, j * P:(j + 1) * P], qk[r, o, 1, 0:S],
                                      start=True, stop=True)
                        last.then_inc(scored, 1)

                    def turn(j):
                        pe.wait_ge(mixed, q0 + j + 1)
                        after(pe, turned_copied, q0 + j)
                        for kb in range(B):
                            last = nc.tensor.transpose(ps[:, 5, kb * P:(kb + 1) * P],
                                                       amix[:, j % 2, kb * P:(kb + 1) * P], ident)
                        last.then_inc(turned, 1)

                    def project(x, i, bank, free_sem, free_n):
                        after(pe, free_sem, free_n)
                        if i == 0:
                            pe.wait_ge(unit_in[u % 2], 16 * (u // 2 + 1) + 8 * (h - par_))
                        if x != "v":
                            product(bank, w[i], hbuf).then_inc(proj[x], 1)
                        else:
                            for t in range(B):
                                for k in range(KC):
                                    last = mm(ps[:, bank, t * P:(t + 1) * P], hbuf[:, k, t * P:(t + 1) * P],
                                              w[i][:, k, :], start=(k == 0), stop=(k == KC - 1))
                            last.then_inc(proj[x], 1)

                    def rotate(x, i):
                        pe.wait_ge(copied[x], hg + 1)
                        if x == "k":
                            pe.wait_ge(roped["q"], hg + 1)
                        else:
                            after(pe, roped["k"], hg)
                        mm(ps[:, 2, 0:S], rot, qkraw[:, i, 0:S], start=True, stop=True).then_inc(rotated[x], 1)

                    if do_att:
                        scores(0)
                    if do_proj:
                        project("q", 0, 0, copied["v"], hg)
                    if do_att:
                        turn(0)
                        scores(1)
                    if do_proj:
                        rotate("q", 0)
                        project("k", 1, 1, o_copied, hg - 1)
                    if do_att:
                        turn(1)
                        if B > 2:
                            scores(2)
                    if do_proj:
                        rotate("k", 1)
                        project("v", 2, 0, copied["q"], hg + 1)
                    if do_att:
                        for j in range(2, B):
                            turn(j)
                            if j + 1 < B:
                                scores(j + 1)
                        pe.wait_ge(turned_copied, q0 + B)
                        pe.wait_ge(copied["v"], hg)
                        if do_proj:
                            pe.wait_ge(copied["k"], hg + 1)
                        for kb in range(B):
                            last = mm(ps[:, 1, 0:S], vh[:, 1 - par_, kb * P:(kb + 1) * P],
                                      amix_t[:, kb, 0:S], start=(kb == 0), stop=(kb == B - 1))
                        last.then_inc(pv_done, 1)

                head(0, 0, True, False)
                head(1, 1, True, True)
                with pe.Fori(0, HEADS // 2 - 1) as i:
                    head(2 * i + 2, 0, True, True)
                    head(2 * i + 3, 1, True, True)
                head(HEADS, 0, False, True)

                for h in range(HEADS):
                    pe.wait_ge(sq_ready, nsq + 8 + h + 1)
                    pe.wait_ge(var_ready, 10 * g + 1 + h)
                    mm(ps[:, 2, 0:S], ones, sq[:, h % 2, 0:S], start=True, stop=True).then_inc(sq_summed, 1)
                for c in range(4):
                    n = 4 * g + c
                    pe.wait_ge(pool_diff, n + 1)
                    if c < 2:
                        pe.wait_ge(o_copied, 8 * (g + 1))
                    else:
                        pe.wait_ge(mix_copied, n - 1)
                    mm(ps[:, c % 2, 0:S], poolw[:, c, :], pdif[:, c, 0:S], start=True,
                       stop=True).then_inc(mix_done, 1)
                pe.wait_ge(mix_copied, 4 * g + 4)
                pe.wait_ge(o_normed, 8 * g + 8)

                def chunk(c, j):
                    u = b + 9 + j
                    pe.wait_ge(unit_in[u % 2], 16 * (u // 2 + 1) + 8 * (c - j))
                    after(pe, z_ready, c + (8 * g - 1) if not isinstance(c, int) else (8 * g + c - 1) * (c > 1))
                    product(4 * j, wtile(u, 0), hbuf)
                    product(4 * j + 1, wtile(u, 1), hbuf)
                    product(4 * j + 2, wtile(u, 2), obuf)
                    product(4 * j + 3, wtile(u, 3), pdif, 4).then_inc(z_done, 1)

                chunk(0, 0)
                chunk(1, 1)
                with pe.Fori(1, KC // 2) as i:
                    for j in range(2):
                        chunk(2 * i + j, j)
                pe.wait_ge(z_ready, 8 * g + 8)

                for c in range(KC):
                    u = b + 17 + c // 4
                    if c % 4 == 0:
                        unit_landed(pe, u)
                    if c >= 2:
                        pe.wait_ge(x1_ready, 8 * g + c - 1)
                    product(c % 2, wtile(u, c % 4), zbuf).then_inc(out_done, 1)
                pe.wait_ge(x1_ready, 8 * g + 8)
                for t in range(B):
                    after(pe, x1_copied, tbase[g] + t)
                    for k in range(KC):
                        last = nc.tensor.transpose(ps[:, 6 + k // 4, (k % 4) * P:(k % 4 + 1) * P],
                                                   hbuf[:, k, t * P:(t + 1) * P], ident)
                    last.then_inc(x1_turned, 1)
                sum_squares(nsq + 16)
                pe.wait_ge(norm_done, 2 * g + 2)
                for k in range(KC):
                    pe.wait_ge(diag_ready, KC * g + k + 1)
                    mm(ps[:, 6 + k // 4, (k % 4) * P:(k % 4 + 1) * P], ones, diag[:, k % 2, :],
                       start=True, stop=True).then_inc(gt2_done, 1)

                pe.wait_ge(keys_in, 16 * (g + 1))

                def key_scores(h):
                    n = 8 * g + h
                    pe.wait_ge(pq_copied, n + 1)
                    if h >= 2:
                        pe.wait_ge(keyed_copied, n - 1)
                    for t in range(B):
                        bank = 2 + 2 * (h % 2) + t // 2
                        o = (t % 2) * 2 * P
                        last = mm(ps[:, bank, o:o + 2 * P], qh[:, h % 2, t * P:(t + 1) * P], keybd[:, h, :],
                                  start=True, stop=True)
                    last.then_inc(keyed, 1)

                for h in range(HEADS):
                    u = b + 19 + h // 4
                    if h % 4 == 0:
                        unit_landed(pe, u)
                    if h >= 2:
                        pe.wait_ge(pq_copied, 8 * g + h - 1)
                    product(h % 2, wtile(u, h % 4), obuf).then_inc(pq_done, 1)
                    if h:
                        key_scores(h - 1)
                key_scores(HEADS - 1)

            all_done(pe)

            def products(out, pairs, start, stop):
                for x, (a, b_) in enumerate(pairs):
                    last = mm(out, a, b_, start=start and x == 0, stop=stop and x == len(pairs) - 1,
                              skip_group_check=True)
                return last

            def score(k, t):
                pe.wait_ge(u_lo_ready, k + 1)
                after(pe, gelu_done, k - 1)
                pairs = []
                for c in range(KC):
                    uh, ul = u_hi[:, t % 2, c, :], u_lo[:, t % 2, c, :]
                    pairs += [(uh, h_hi[:, c, :]), (uh, h_lo[:, c, :]), (ul, h_hi[:, c, :])]
                products(ps[:, t % 2, 0:TOK], pairs, True, True).then_inc(s_done, 1)

            def combine(k, t, start=False, stop=False):
                pe.wait_ge(v_lo_ready, k + 1)
                pe.wait_ge(c_lo_ready, k + 1)
                j = t % 2
                for tb in range(2):
                    ch, cl = c_hi[:, j, tb * P:(tb + 1) * P], c_lo[:, j, tb * P:(tb + 1) * P]
                    for f in range(2):
                        vh_, vl = v_hi[:, j, f * 512:(f + 1) * 512], v_lo[:, j, f * 512:(f + 1) * 512]
                        last = products(ps[:, 4 + 2 * tb + f, :], [(ch, vh_), (ch, vl), (cl, vh_)], start, stop)
                last.then_inc(v_done, 1)

            def gate_step(s, t):
                pe.wait_ge(hot_ready, s + 1)
                after(pe, g_copied, s - 1)
                j = t % 2
                for x in range(4):
                    last = products(ps[:, 2 + j, x * P:(x + 1) * P],
                                    [(hot1[:, j, x, :], hot2h[:, j, x, :]), (hot1[:, j, x, :], hot2l[:, j, x, :])],
                                    True, True)
                last.then_inc(g_done, 1)

            for n in range(-1, PASSES):
                nxt = n + 1 if n + 1 < PASSES else None

                def body(i, building=False, first=False):
                    for t in range(4):
                        k = 4 * i + (t + P * n)
                        if n >= 0:
                            score(k, t)
                        if n >= 0 and not (first and t == 0):
                            if first and t == 1:
                                after(pe, acc_read, n)
                            combine(k - 1, t + 3, start=first and t == 1)
                        if building:
                            gate_step(4 * i + (STEPS * (nxt - 1) + t), t)

                if n >= 0:
                    pe.wait_ge(h_lo_ready, n + 1)
                    body(0, first=True)
                    with pe.Fori(1, 16) as i:
                        body(i)
                if nxt is not None:
                    pe.wait_ge(sel_ready, nxt + 1)
                    after(pe, g_copied, STEPS * nxt)
                    after(pe, y_squared, 2 * n)
                    for tb in range(2):
                        for x in range(3):
                            last = nc.tensor.transpose(ps[:, 2 + tb, x * P:(x + 1) * P],
                                                       sel[:, x, tb * P:(tb + 1) * P], ident)
                    last.then_inc(sel_turned, 1)
                    pe.wait_ge(sel_copied, nxt + 1)
                    body(16, building=True)
                    with pe.Fori(17, 32) as i:
                        body(i, building=True)
                else:
                    with pe.Fori(16, 32) as i:
                        body(i)
                if n >= 0:
                    combine(P * (n + 1) - 1, 3, stop=True)

        @block.scalar
        def _(act):
            A = nc.scalar.activation
            act.wait_ge(consts_in, 32)
            cs = par[:, V_C:V_C + 16].rearrange("p (k g) -> p k g", g=2)
            A(silu_c[:], cs, ACT.Sigmoid).then_inc(silu_a, 1)
            act.wait_ge(lam_dot, 1)
            A(small[:, 2:4], small[:, 0:2], ACT.Exp).then_inc(lam_exp, 1)

            for g, S in enumerate(SEQS):
                B = S // P
                if g:
                    all_done(act)
                nsq = g * 24

                def squares(n0):
                    for c in range(KC):
                        if c >= 2:
                            act.wait_ge(sq_summed, n0 + c - 1)
                        A(sq[:, c % 2, 0:S], hbuf[:, c, 0:S], ACT.Square).then_inc(sq_ready, 1)

                act.wait_ge(group_in, 48 * (g + 1))
                squares(nsq)
                act.wait_ge(var_ready, 10 * g + 1)
                A(rstd[:, 0:S], rstd[:, 0:S], ACT.Sqrt).then_inc(rstd_ready, 1)
                for c in range(4):
                    act.wait_ge(p_done, 4 * g + c + 1)
                    nc.scalar.copy(pbuf[:, c, PAD:PAD + S], ps[:, c % 2, 0:S]).then_inc(p_copied, 1)

                def head(h, par_, do_proj, do_att):
                    hg = 8 * g + h
                    q0 = qbase[g] + (h - 1) * B

                    def expo(j):
                        pe_ = j % 2
                        act.wait_ge(maxed, q0 + j + 1)
                        after(act, mixed, q0 + j - 1)
                        for m in range(2):
                            last = A(expd[:, pe_, m, 0:S], ps[:, 3 + m, 0:S], ACT.Exp,
                                     bias=small[:, 4 + 2 * pe_ + m:5 + 2 * pe_ + m], scale=HALF ** -0.5,
                                     accum_out=small[:, 8 + 2 * pe_ + m:9 + 2 * pe_ + m])
                        last.then_inc(expd_ready, 1)

                    def turned_out(j):
                        act.wait_ge(turned, q0 + j + 1)
                        if j == 0:
                            after(act, pv_done, hg - 1)
                        nc.scalar.copy(amix_t[:, 0:B, j * P:(j + 1) * P],
                                       ps[:, 5, 0:S].rearrange("p (b n) -> p b n", n=P)).then_inc(turned_copied, 1)

                    def raw_out(x, i, bank):
                        act.wait_ge(proj[x], hg + 1)
                        if x == "v":
                            after(act, pv_done, hg - 1)
                            nc.scalar.copy(vh[:, par_, 0:S], ps[:, bank, 0:S]).then_inc(copied[x], 1)
                        else:
                            after(act, roped[x], hg)
                            nc.scalar.copy(qkraw[:, i, 0:S], ps[:, bank, 0:S]).then_inc(copied[x], 1)

                    if do_att:
                        expo(0)
                    if do_proj:
                        raw_out("q", 0, 0)
                    if do_att:
                        turned_out(0)
                        expo(1)
                    if do_proj:
                        raw_out("k", 1, 1)
                    if do_att:
                        turned_out(1)
                        if B > 2:
                            expo(2)
                    if do_proj:
                        raw_out("v", 2, 0)
                    if do_att:
                        for j in range(2, B):
                            turned_out(j)
                            if j + 1 < B:
                                expo(j + 1)
                        act.wait_ge(pv_done, hg)
                        hh = h - 1
                        dst = (obuf[:, hh, 0:S] if isinstance(hh, int)
                               else obuf[:, bass.ds(hh, 1), 0:S].rearrange("p a s -> p (a s)"))
                        nc.scalar.copy(dst, ps[:, 1, 0:S]).then_inc(o_copied, 1)

                head(0, 0, True, False)
                head(1, 1, True, True)
                with act.Fori(0, HEADS // 2 - 1) as i:
                    head(2 * i + 2, 0, True, True)
                    head(2 * i + 3, 1, True, True)
                head(HEADS, 0, False, True)
                act.drain()
                for h in range(HEADS):
                    if h >= 2:
                        act.wait_ge(sq_summed, nsq + 8 + h - 1)
                    A(sq[:, h % 2, 0:S], obuf[:, h, 0:S], ACT.Square).then_inc(sq_ready, 1)
                    if h:
                        act.wait_ge(var_ready, 10 * g + 1 + h)
                        A(orstd[(h - 1) % 2][:, 0:S], orstd[(h - 1) % 2][:, 0:S], ACT.Sqrt).then_inc(rstd_ready, 1)
                act.wait_ge(var_ready, 10 * g + 1 + HEADS)
                A(orstd[1][:, 0:S], orstd[1][:, 0:S], ACT.Sqrt).then_inc(rstd_ready, 1)
                for c in range(4):
                    act.wait_ge(mix_done, 4 * g + c + 1)
                    A(pdif[:, c, 0:S], ps[:, c % 2, 0:S], ACT.Copy,
                      scale=par[:, V_PSC + c:V_PSC + c + 1]).then_inc(mix_copied, 1)
                for c in range(KC):
                    act.wait_ge(z_done, 8 * g + c + 1)
                    if c >= 2:
                        act.wait_ge(z_ready, 8 * g + c - 1)
                    for m in range(2):
                        last = A(expd[:, c % 2, m, 0:S], ps[:, 4 * (c % 2) + m, 0:S], ACT.Sigmoid,
                                 bias=par[:, V_BGATE + 8 * m + c:V_BGATE + 8 * m + c + 1])
                    last.then_inc(sig_done, 1)
                for t in range(B):
                    act.wait_ge(x1_turned, tbase[g] + t + 1)
                    if t >= 2:
                        act.wait_ge(x1_stored[t % 2], 16 * ((tbase[g] + t) // 2))
                    if t == 0:
                        act.wait_ge(x1_ready, 8 * g + 8)
                    nc.scalar.copy(x1tok[:, t % 2, :].rearrange("p (a n) -> p a n", a=2),
                                   ps[:, 6:8, :]).then_inc(x1_copied, 1)
                squares(nsq + 16)
                act.wait_ge(var_ready, 10 * g + 10)
                A(rstd[:, 0:S], rstd[:, 0:S], ACT.Sqrt).then_inc(rstd_ready, 1)
                act.wait_ge(gt2_done, KC * (g + 1))
                nc.scalar.copy(gt2row.rearrange("p (a n) -> p a n", a=2), ps[:, 6:8, :]).then_inc(gt2_copied, 1)
                for h in range(HEADS + 1):
                    if h < HEADS:
                        act.wait_ge(pq_done, 8 * g + h + 1)
                        if h >= 2:
                            act.wait_ge(keyed, 8 * g + h - 1)
                        nc.scalar.copy(qh[:, h % 2, 0:S], ps[:, h % 2, 0:S]).then_inc(pq_copied, 1)
                    if h:
                        m = h - 1
                        act.wait_ge(keyed, 8 * g + h)
                        if m >= 2:
                            act.wait_ge(scores_stored[m % 2], 16 * (4 * g + m // 2))
                        bank = 2 + 2 * (m % 2)
                        nc.scalar.copy(sc[:, m % 2, 0:2 * S].rearrange("p (a n) -> p a n", n=512),
                                       ps[:, bank:bank + S // 256, :]).then_inc(keyed_copied, 1)

            all_done(act)
            copy = nc.scalar.copy

            def flat(t):
                return t.rearrange("p a b -> p (a b)")

            def split_u(k, i, n, t):
                act.wait_ge(raw_in[t], 16 * i + (16 * (P // 4) * n + 16))
                after(act, s_done, k - 1)
                copy(flat(u_hi[:, t % 2]), raw[:, t, 0:D]).then_inc(u_hi_ready, 1)

            def split_v(k, t):
                after(act, v_done, k - 1)
                copy(v_hi[:, t % 2, :], raw[:, t, D:2 * D]).then_inc(v_hi_ready, 1)

            def coefficients(k, t):
                j = t % 2
                act.wait_ge(s_done, k + 1)
                after(act, c_lo_ready, k - 1)
                A(coef[:, j, :], ps[:, j, 0:TOK], ACT.Gelu).then_inc(gelu_done, 1)
                act.wait_ge(coef_ready, k + 1)
                after(act, v_done, k - 1)
                copy(c_hi[:, j, :], coef[:, j, :]).then_inc(c_hi_ready, 1)

            def norm_y(n):
                for j in range(2):
                    m = 2 * n + j
                    act.wait_ge(y_ready, m + 1)
                    A(ps[:, 2:4, :], f_y[:, j, :].rearrange("p (a n) -> p a n", a=2), ACT.Square,
                      accum_out=small[:, 12:13]).then_inc(y_squared, 1)
                    act.wait_ge(y_var, m + 1)
                    A(small[:, 13:14], small[:, 13:14], ACT.Sqrt).then_inc(y_rstd, 1)

            for n in range(-1, PASSES):
                nxt = n + 1 if n + 1 < PASSES else None

                def copy_gates(i, q, t):
                    act.wait_ge(g_done, 4 * i + (STEPS * (nxt - 1) + t + 1))
                    col = 16 * i + (STAGE * (q % 2) + 4 * t - 16 * (16 + 4 * q))
                    copy(staged[:, :, bass.ds(col, 4)],
                         ps[:, 2 + t % 2, :].rearrange("p (t k) -> p k t", t=4)).then_inc(g_copied, 1)

                def body(i, q=None, first=False, opens=False):
                    for t in range(4):
                        k = 4 * i + (t + P * n)
                        if n >= 0:
                            split_u(k, i, n, t)
                        if q is not None:
                            if t:
                                copy_gates(i, q, t - 1)
                            elif not opens:
                                copy_gates(i - 1, q, 3)
                        if n >= 0:
                            if not (first and t == 0):
                                coefficients(k - 1, t + 3)
                            split_v(k, t)

                if n >= 0:
                    body(0, first=True)
                    if n:
                        norm_y(n - 1)
                    with act.Fori(1, 16) as i:
                        body(i)
                if nxt is not None:
                    act.wait_ge(shifted, nxt + 1)
                    A(sel[:, 2, :], sel[:, 2, :], ACT.Exp).then_inc(exped, 1)
                    act.wait_ge(sel_turned, nxt + 1)
                    turned_ = ps[:, 2:4, 0:3 * P].rearrange("p b (x n) -> p x b n", x=3)
                    for x in range(3):
                        last = copy(sel_t[:, x, :].rearrange("p (b n) -> p b n", b=2), turned_[:, x])
                    last = copy(gate_hi[:].rearrange("p (b n) -> p b n", b=2), turned_[:, 2])
                    last.then_inc(sel_copied, 1)
                    for q in range(4):
                        Q = 4 * nxt + q
                        if Q >= 2:
                            act.wait_ge(gates_stored[q % 2], 16 * (Q // 2))
                        body(16 + 4 * q, q=q, opens=True)
                        with act.Fori(17 + 4 * q, 20 + 4 * q) as i:
                            body(i, q=q)
                        copy_gates(19 + 4 * q, q, 3)
                        act.wait_ge(g_copied, 16 * (Q + 1))
                        cols = slice(STAGE * (q % 2), STAGE * (q % 2 + 1))
                        act.dma_start(gate_dram[nxt].rearrange("j p t -> p j t")[:, :, STAGE * q:STAGE * (q + 1)],
                                      staged[:, :, cols]).then_inc(gates_stored[q % 2], 16)
                else:
                    with act.Fori(16, 32) as i:
                        body(i)
                if n >= 0:
                    coefficients(P * (n + 1) - 1, 3)
                if nxt is not None:
                    act.wait_ge(h_in, 16 * (nxt + 1))
                    after(act, s_done, P * nxt)
                    copy(flat(h_hi[:]), flat(f_y[:])).then_inc(h_hi_ready, 1)
            norm_y(PASSES - 1)

        @block.vector
        def _(dve):
            V = nc.vector
            tt, ts, stt = V.tensor_tensor, V.tensor_scalar, V.scalar_tensor_tensor
            dve.wait_ge(consts_in, 32)
            cs = par[:, V_C:V_C + 16].rearrange("p (k g) -> p k g", g=2)
            lamv = par[:, V_LAM:V_LAM + 256].rearrange("p (m k n) -> p m k n", m=2, k=2)
            tt(rtmp[:, 0:128].rearrange("p (m n) -> p m n", m=2), lamv[:, :, 0, :], lamv[:, :, 1, :], ALU.mult)
            dve.drain()
            V.tensor_reduce(small[:, 0:2], rtmp[:, 0:128].rearrange("p (m n) -> p m n", m=2), AX.X,
                            ALU.add).then_inc(lam_dot, 1)
            dve.wait_ge(silu_a, 1)
            tt(silu_c[:], silu_c[:], cs, ALU.mult).then_inc(silu_b, 1)
            dve.wait_ge(lam_exp, 1)
            stt(out=nlam[:], in0=small[:, 3:4], scalar=-LAM_INIT, in1=small[:, 2:3], op0=ALU.add, op1=ALU.subtract)
            ts(gsub[:], par[:, V_GSUB:V_GSUB + 1], 1.0 - LAM_INIT, None, ALU.mult)
            dve.wait_ge(ada_done, UNITS_ADA)
            tt(mod[:], ps[:, 0, 0:96].rearrange("p (c g) -> p c g", g=2),
               par[:, V_BADA:V_BADA + 48].unsqueeze(2).broadcast_to((P, 48, 2)), ALU.add)
            dve.drain()
            for g in range(2):
                for n, v in enumerate((V_G1, V_G2)):
                    stt(out=scl[:, g, n, :], in0=mod[:, 24 * n + 8:24 * n + 16, g], scalar=1.0,
                        in1=par[:, v:v + 8], op0=ALU.add, op1=ALU.mult)

            for g, S in enumerate(SEQS):
                B = S // P
                nsq = g * 24
                if g:
                    all_done(dve)

                def inverse(dst, src, n):
                    ts(dst, src, 1.0 / n, EPS, ALU.mult, ALU.add)
                    dve.drain()
                    return V.reciprocal(dst, dst)

                def norm(n, dst):
                    dve.wait_ge(sq_summed, nsq + 16 * n + 8)
                    inverse(rstd[:, 0:S], ps[:, 2, 0:S], D).then_inc(var_ready, 1)
                    dve.wait_ge(rstd_ready, 10 * g + 9 * n + 1)
                    for c in range(KC):
                        tt(dst[:, c, 0:S], hbuf[:, c, 0:S], rstd[:, 0:S], ALU.mult)
                    dve.drain()
                    for c in range(KC):
                        last = ts(dst[:, c, 0:S], dst[:, c, 0:S], scl[:, g, n, c:c + 1],
                                  mod[:, 24 * n + c, g:g + 1], ALU.mult, ALU.add)
                    last.then_inc(norm_done, 1)

                norm(0, hbuf)

                def head(h, par_, do_proj, do_att):
                    hg = 8 * g + h
                    q0 = qbase[g] + (h - 1) * B

                    def maxima(j):
                        pe_ = j % 2
                        nm = small[:, 4 + 2 * pe_:6 + 2 * pe_]
                        dve.wait_ge(scored, q0 + j + 1)
                        V.tensor_reduce(nm, ps[:, 3:5, 0:S], AX.X, ALU.max)
                        dve.drain()
                        ts(nm, nm, -HALF ** -0.5, None, ALU.mult).then_inc(maxed, 1)

                    def mix(j):
                        pe_ = j % 2
                        zs = small[:, 8 + 2 * pe_:10 + 2 * pe_]
                        dve.wait_ge(expd_ready, q0 + j + 1)
                        after(dve, turned, q0 + j - 1)
                        V.reciprocal(zs, zs)
                        dve.drain()
                        ts(expd[:, pe_, 1, 0:S], expd[:, pe_, 1, 0:S], zs[:, 1:2], nlam[:, 0:1], ALU.mult, ALU.mult)
                        dve.drain()
                        stt(out=amix[:, pe_, 0:S], in0=expd[:, pe_, 0, 0:S], scalar=zs[:, 0:1],
                            in1=expd[:, pe_, 1, 0:S], op0=ALU.mult, op1=ALU.add).then_inc(mixed, 1)

                    def rope_(x, i):
                        dst = qk[:, par_, i, 0:S]
                        dve.wait_ge(copied[x], hg + 1)
                        after(dve, scored, q0)
                        tt(dst, qkraw[:, i, 0:S], cossin[:, 0, 0:S], ALU.mult)
                        dve.wait_ge(rotated[x], hg + 1)
                        tt(rtmp[:, 0:S], ps[:, 2, 0:S], cossin[:, 1, 0:S], ALU.mult)
                        dve.drain()
                        tt(dst, dst, rtmp[:, 0:S], ALU.add).then_inc(roped[x], 1)

                    if do_att:
                        maxima(0)
                        mix(0)
                        maxima(1)
                    if do_proj:
                        rope_("q", 0)
                    if do_att:
                        mix(1)
                        if B > 2:
                            maxima(2)
                    if do_proj:
                        rope_("k", 1)
                    if do_att:
                        for j in range(2, B):
                            mix(j)
                            if j + 1 < B:
                                maxima(j + 1)

                head(0, 0, True, False)
                head(1, 1, True, True)
                with dve.Fori(0, HEADS // 2 - 1) as i:
                    head(2 * i + 2, 0, True, True)
                    head(2 * i + 3, 1, True, True)
                head(HEADS, 0, False, True)

                dve.drain()
                for h in range(HEADS):
                    dve.wait_ge(sq_summed, nsq + 8 + h + 1)
                    inverse(orstd[h % 2][:, 0:S], ps[:, 2, 0:S], P).then_inc(var_ready, 1)
                    dve.wait_ge(rstd_ready, 10 * g + 2 + h)
                    stt(out=obuf[:, h, 0:S], in0=obuf[:, h, 0:S], scalar=gsub[:, 0:1], in1=orstd[h % 2][:, 0:S],
                        op0=ALU.mult, op1=ALU.mult).then_inc(o_normed, 1)
                for c in range(KC):
                    k = 4 * (c % 2)
                    dve.wait_ge(sig_done, 8 * g + c + 1)
                    tt(zbuf[:, c, 0:S], ps[:, k + 3, 0:S], expd[:, c % 2, 0, 0:S], ALU.mult)
                    att = expd[:, c % 2, 1, 0:S]
                    tt(att, ps[:, k + 2, 0:S], att, ALU.mult)
                    dve.drain()
                    tt(zbuf[:, c, 0:S], zbuf[:, c, 0:S], att, ALU.add).then_inc(z_ready, 1)
                dve.wait_ge(x_again, 16 * (g + 1))
                for c in range(KC):
                    dve.wait_ge(out_done, 8 * g + c + 1)
                    stt(out=hbuf[:, c, 0:S], in0=ps[:, c % 2, 0:S], scalar=mod[:, 16 + c, g:g + 1],
                        in1=obuf[:, c, 0:S], op0=ALU.mult, op1=ALU.add).then_inc(x1_ready, 1)
                dve.drain()
                norm(1, obuf)
                for k in range(KC):
                    if k >= 2:
                        dve.wait_ge(gt2_done, KC * g + k - 1)
                    ts(diag[:, k % 2, :], ident, mod[:, 40 + k, g:g + 1], None, ALU.mult).then_inc(diag_ready, 1)

            all_done(dve)
            iota16 = iota[:, 0:TOPK]
            square = (P, TOPK, TOPK)

            def flat(t):
                return t.rearrange("p a b -> p (a b)")

            def top16(src, spare_, val, idx):
                V.max(val[:, 0:8], src)
                dve.drain()
                V.max_index(idx[:, 0:8], val[:, 0:8], src)
                last = V.match_replace(spare_, val[:, 0:8], src, NEG)
                dve.drain()
                V.max(val[:, 8:16], spare_)
                dve.drain()
                V.max_index(idx[:, 8:16], val[:, 8:16], spare_)
                return last

            def search(nxt, i, part):
                if part == 0:
                    dve.wait_ge(score_loaded, 16 * i + (256 * nxt + 16))
                    V.tensor_copy(jf[:, 0, 0:1], score_in[:, 0, 0:1])
                    dve.drain()
                if part < 2:
                    top16(score_in[:, part, :], spare[:, part, :], best[:, part, :], besti[:, part, :])
                    if part == 1:
                        dve.drain()
                        V.tensor_copy(bestf[:], besti[:]).then_inc(score_free, 1)
                    dve.drain()
                elif part == 2:
                    tt(cand[:, 0], best[:, 0, :].unsqueeze(2).broadcast_to(square),
                       best[:, 1, :].unsqueeze(1).broadcast_to(square), ALU.add)
                    dve.drain()
                    top16(flat(cand[:, 0]), flat(cand[:, 1]), pair[:], jbest[:])
                    dve.drain()
                    ts(jhalf[:, 0, :], jbest[:], 4, None, ALU.logical_shift_right)
                    ts(jhalf[:, 1, :], jbest[:], TOPK - 1, None, ALU.bitwise_and)
                    dve.drain()
                    V.tensor_copy(jf[:], jhalf[:])
                    dve.drain()
                else:
                    V.tensor_copy(sel[:, 2, bass.ds(16 * i, TOPK)], pair[:])
                    for x in range(2):
                        tt(cand[:, x], jf[:, x, :].unsqueeze(2).broadcast_to(square),
                           iota16.unsqueeze(1).broadcast_to(square), ALU.is_equal)
                    dve.drain()
                    for x in range(2):
                        tt(cand[:, x], cand[:, x], bestf[:, x, :].unsqueeze(1).broadcast_to(square), ALU.mult)
                    dve.drain()
                    for x in range(2):
                        V.tensor_reduce(sel[:, x, bass.ds(16 * i, TOPK)], cand[:, x], AX.X, ALU.add)
                    dve.drain()

            def hot_step(s, tok, t):
                after(dve, g_done, s - 1)
                j = t % 2
                for x in range(4):
                    col = bass.ds(tok + x, 1)
                    ts(hot1[:, j, x, :], iota, sel_t[:, 0, col], None, ALU.is_equal)
                    ts(hot2h[:, j, x, :], iota, sel_t[:, 1, col], gate_hi[:, col].bitcast(F32),
                       ALU.is_equal, ALU.mult)
                    last = ts(hot2l[:, j, x, :], iota, sel_t[:, 1, col], gate_lo[:, col], ALU.is_equal, ALU.mult)
                last.then_inc(hot_ready, 1)

            def split_u(k, t):
                dve.wait_ge(u_hi_ready, k + 1)
                tt(flat(u_lo[:, t % 2]), raw[:, t, 0:D], flat(u_hi[:, t % 2].bitcast(F32)),
                   ALU.subtract).then_inc(u_lo_ready, 1)

            def coefficients(k, loaded, t):
                j = t % 2
                dve.wait_ge(gelu_done, k + 1)
                dve.wait_ge(gate_loaded[t % 4], loaded)
                tt(coef[:, j, :], coef[:, j, :], gate_in[:, t % 4, :], ALU.mult).then_inc(coef_ready, 1)
                dve.wait_ge(c_hi_ready, k + 1)
                tt(c_lo[:, j, :], coef[:, j, :], c_hi[:, j, :].bitcast(F32), ALU.subtract).then_inc(c_lo_ready, 1)

            def norm_y(n):
                dve.wait_ge(fin_in, 16 + 48 * (n + 1))
                for j in range(2):
                    m = 2 * n + j
                    y = f_y[:, j, :]
                    tt(y, y, f_x1[:, j, :], ALU.add).then_inc(y_ready, 1)
                    dve.wait_ge(y_squared, m + 1)
                    inverse(small[:, 13:14], small[:, 12:13], D).then_inc(y_var, 1)
                    dve.wait_ge(y_rstd, m + 1)
                    stt(out=y, in0=y, scalar=small[:, 13:14], in1=f_gf[:], op0=ALU.mult,
                        op1=ALU.mult).then_inc(y_final, 1)

            for n in range(-1, PASSES):
                nxt = n + 1 if n + 1 < PASSES else None

                def body(i, searching=False, building=False, first=False):
                    for t in range(4):
                        k = 4 * i + (t + P * n)
                        if n >= 0:
                            split_u(k, t)
                            if not (first and t == 0):
                                coefficients(k - 1, 16 * i + (16 * (P // 4) * n + (16 if t else 0)), t + 3)
                        if searching:
                            search(nxt, i, t)
                        if building:
                            hot_step(4 * i + (STEPS * (nxt - 1) + t), 16 * i + (4 * t - 256), t)

                if n >= 0:
                    body(0, searching=nxt is not None, first=True)
                    if n:
                        norm_y(n - 1)
                with dve.Fori(max(0, min(n + 1, 1)), 16) as i:
                    body(i, searching=nxt is not None)
                if nxt is not None:
                    v = sel[:, 2, :].rearrange("p (h k) -> p h k", k=TOPK)
                    per_head = gsum[:].unsqueeze(2).broadcast_to(square)
                    V.tensor_copy(gsum[:], v[:, :, 0])
                    dve.drain()
                    tt(v, v, per_head, ALU.subtract).then_inc(shifted, 1)
                    dve.wait_ge(exped, nxt + 1)
                    V.tensor_reduce(gsum[:], v, AX.X, ALU.add)
                    dve.drain()
                    V.reciprocal(gsum[:], gsum[:])
                    dve.drain()
                    tt(v, v, per_head, ALU.mult).then_inc(sel_ready, 1)
                    dve.wait_ge(sel_copied, nxt + 1)
                    tt(gate_lo[:], sel_t[:, 2, :], gate_hi[:].bitcast(F32), ALU.subtract)
                    dve.drain()
                    body(16, building=True)
                    with dve.Fori(17, 32) as i:
                        body(i, building=True)
                else:
                    with dve.Fori(16, 32) as i:
                        body(i)
                if n >= 0:
                    coefficients(P * (n + 1) - 1, 16 * (P // 4) * (n + 1), 3)
                if nxt is not None:
                    dve.wait_ge(h_hi_ready, nxt + 1)
                    tt(flat(h_lo[:]), flat(f_y[:]), flat(h_hi[:].bitcast(F32)), ALU.subtract).then_inc(h_lo_ready, 1)
                if n >= 0:
                    dve.wait_ge(v_done, P * (n + 1))
                    dve.wait_ge(fin_in, 16 + 48 * (n + 1))
                    dve.drain()
                    for j in range(2):
                        last = tt(f_y[:, j, :].rearrange("p (a n) -> p a n", a=2), ps[:, 4 + 2 * j:6 + 2 * j, :],
                                  f_gt2[:].rearrange("p (a n) -> p a n", a=2), ALU.mult)
                    last.then_inc(acc_read, 1)
                    dve.drain()
            norm_y(PASSES - 1)

        @block.gpsimd
        def _(pool):
            G = nc.gpsimd
            for g, S in enumerate(SEQS):
                if g:
                    all_done(pool)
                L = S + 2 * PAD
                G.memset(pbuf[:, :, 0:PAD], 0.0)
                G.memset(pbuf[:, :, PAD + S:L], 0.0)
                for c, w in enumerate(WINDOWS):
                    pool.wait_ge(p_copied, 4 * g + c + 1)
                    src, lo = pbuf[:, c, :], 0
                    for n in range(c + 1):
                        d = max(1, 2 ** n // 2)
                        dst = ptmp[:, n % 2, :]
                        lo, back, ahead = (1, 1, 0) if n == 0 else (lo + d, d, d)
                        pool.drain()
                        G.tensor_tensor(dst[:, lo:L - lo], src[:, lo - back:L - lo - back],
                                        src[:, lo + ahead:L - lo + ahead], ALU.add)
                        src = dst
                    pool.drain()
                    mean = src[:, PAD:PAD + S]
                    G.tensor_scalar(mean, mean, 1.0 / w, None, ALU.mult)
                    pool.drain()
                    G.tensor_tensor(mean[:, 0:PAD], mean[:, 0:PAD], edge[:, c, 0:PAD], ALU.mult)
                    G.tensor_tensor(mean[:, S - PAD:S], mean[:, S - PAD:S], edge[:, c, PAD:2 * PAD], ALU.mult)
                    pool.drain()
                    G.tensor_tensor(pdif[:, c, 0:S], mean, pbuf[:, c, PAD:PAD + S], ALU.subtract).then_inc(pool_diff, 1)
            all_done(pool)
            for n in range(PASSES):
                with pool.Fori(0, P // 4) as i:
                    for t in range(4):
                        pool.wait_ge(v_hi_ready, 4 * i + (P * n + t + 1))
                        G.tensor_tensor(v_lo[:, t % 2, :], raw[:, t, D:2 * D], v_hi[:, t % 2, :].bitcast(F32),
                                        ALU.subtract).then_inc(v_lo_ready, 1)


def shape_constants():
    c = np.zeros((P, C_N), np.float32)
    c[:, C_ID:C_ID + P] = np.eye(P)
    c[:, C_ONE:C_ONE + P] = 1
    for i in range(P):
        if i % HALF < HALF // 2:
            c[i + HALF // 2, C_ROT + i] = -1
        else:
            c[i - HALF // 2, C_ROT + i] = 1
    c[:, C_IOTA:C_IOTA + P] = np.arange(P)
    for n, w in enumerate(WINDOWS):
        for i in range(PAD):
            c[:, C_EDGE + 16 * n + i] = w / (min(i + w // 2, SMAX) - max(i - w // 2, 0))
            back = PAD - i
            c[:, C_EDGE + 16 * n + PAD + i] = w / (min(w // 2, back) + w // 2)
    inv = (1.0 / (10000.0 ** (np.arange(0, HALF, 2, dtype=np.float32) / HALF))).astype(np.float32)
    ang = np.arange(SMAX, dtype=np.float32)[None, :] * np.tile(inv, 4)[:, None]
    rope = np.stack([np.cos(ang), np.sin(ang)], axis=1).astype(np.float32)
    return c, rope


def kernel(**inputs):
    import concourse.bacc as _bacc
    from concourse.bass_utils import run_bass_kernel_spmd as _run

    a = {k: np.asarray(v) for k, v in inputs.items()}
    f = np.float32

    def tiles(w):
        r, n = w.shape
        return w.reshape(r // P, P, n // P, P).transpose(2, 1, 0, 3)

    units = np.zeros((UNITS_ADA + UNITS_GROUP, P, 4, KC, P), f)
    units[:UNITS_ADA] = tiles(a["w_ada"][0]).reshape(UNITS_ADA, 4, P, KC, P).transpose(0, 2, 1, 3, 4)
    u = units[UNITS_ADA:]
    w_in = tiles(a["w_in"][0])
    gate, att, out_, peer = (tiles(a[k][0]) for k in ("w_gate", "w_att_out", "w_out", "w_peer_q"))
    po = tiles(a["w_pool_out"][0])
    for i in range(4):
        u[0][:, i] = w_in[i]
    for h in range(HEADS):
        for i in range(3):
            u[1 + h][:, i] = w_in[4 + 8 * i + h]
    for c in range(KC):
        u[9 + c][:, 0], u[9 + c][:, 1], u[9 + c][:, 2] = gate[c], gate[KC + c], att[c]
        u[9 + c][:, 3, 0:4] = po[c]
        u[17 + c // 4][:, c % 4] = out_[c]
        u[19 + c // 4][:, c % 4] = peer[c]

    def cols(v):
        return v.reshape(-1, P).T

    params = np.zeros((P, V_N), f)
    for at, v in ((V_G1, a["g_norm1"]), (V_G2, a["g_norm2"]), (V_BADA, a["b_ada"]), (V_BGATE, a["b_gate"]),
                  (V_PSC, a["pool_scale"]), (V_GSUB, a["g_sub"])):
        c = cols(v[0])
        params[:, at:at + c.shape[1]] = c
    cc = np.stack([a["c_prompt"][0].reshape(KC, P), a["c_sample"][0].reshape(KC, P)], axis=2)
    params[:, V_C:V_C + 16] = cc.transpose(1, 0, 2).reshape(P, 16)
    params[:, V_LAM:] = np.concatenate([a[k][0] for k in ("lam_q1", "lam_k1", "lam_q2", "lam_k2")])[None, :]
    keys = np.zeros((P, HEADS, 2 * P), f)
    for x in range(2):
        keys[HALF * x:HALF * (x + 1), :, P * x:P * (x + 1)] = a["peer_keys"][0][:, x].transpose(2, 0, 1)
    consts, rope = shape_constants()
    x_t = [a[k][0].T.reshape(KC, P, -1).transpose(1, 0, 2) for k in ("x_prompt", "x_sample")]
    eu = a["peer_u"][0].reshape(P, P, KC, P).transpose(1, 3, 2, 0).reshape(P, P, D)
    ev = a["peer_v"][0].reshape(P, P, D).transpose(1, 0, 2)
    sent = {
        "consts": consts, "params": params, "rope": rope, "keys": keys,
        "pool_w": a["pool_w"][0].transpose(1, 0, 2), "g_final": np.broadcast_to(a["g_final"], (P, D)),
        "x_t0": x_t[0], "x_t1": x_t[1], "weights": units.reshape(-1, P, UNIT),
        "table": np.concatenate([eu, ev], axis=2),
    }
    sent = {"in_" + k: np.ascontiguousarray(v) for k, v in sent.items()}
    nc = _bacc.Bacc("TRN2", target_bir_lowering=False, num_devices=1)
    ap = {k: nc.dram_tensor(k, v.shape, mybir.dt.from_np(v.dtype), kind="ExternalInput").ap() for k, v in sent.items()}
    outs = [nc.dram_tensor("out_%d" % g, (1, S, D), F32, kind="ExternalOutput").ap() for g, S in enumerate(SEQS)]
    build(nc, ap["in_consts"], ap["in_params"], ap["in_rope"], ap["in_keys"], ap["in_pool_w"], ap["in_g_final"],
          [ap["in_x_t0"], ap["in_x_t1"]], ap["in_weights"], ap["in_table"], outs)
    r = _run(nc, [sent], core_ids=[0])
    return tuple(r.results[0]["out_%d" % g] for g in range(2))
```

```python
from contextlib import ExitStack

import numpy as np

import concourse.bass as bass
from concourse import mybir

F32 = mybir.dt.float32
F32R = mybir.dt.float32r
U32 = mybir.dt.uint32
ALU = mybir.AluOpType
ACT = mybir.ActivationFunctionType
AX = mybir.AxisListType

P = 128
D = 1024
KC = D // P
HEADS = 8
HALF = 64
TOPK = 16
SEQS = (256, 512)
SMAX = max(SEQS)
EPS = 1e-6
LAM_INIT = 0.2
WINDOWS = (2, 4, 8, 16)
PAD = 8
LROW = SMAX + 2 * PAD
TOK = 256
PASSES = sum(SEQS) // TOK
STAGE = 64
QUARTERS = TOK // STAGE
EARLY = 8
TILE = KC * P
UNIT = 4 * TILE
UNITS_ADA = 12
ADA_FIRST = 4
UNITS_GROUP = 21
SPLIT_TILES = 4 + 3 * HEADS + 2 * KC
Z_SEARCHES = 3 * (KC // 2 - 1) + 1
ARENA = 26240
NEG = -3.0e38

C_ID, C_ONE, C_ROT, C_IOTA, C_EDGE, C_N = 0, 128, 256, 384, 512, 512 + 4 * 16
V_G1, V_G2, V_BADA, V_BGATE, V_PSC, V_GSUB, V_C, V_LAM, V_N = 0, 8, 16, 64, 80, 84, 85, 101, 101 + 4 * 64


def after(eng, sem, n):
    if isinstance(n, int) and n <= 0:
        return
    eng.wait_ge(sem, n)


def build(nc, consts, params, rope, keys, pool_w, g_final, x_t, weights, table, outs):
    with ExitStack() as ctx:
        def sb(name, shape, dt=F32):
            return ctx.enter_context(nc.sbuf_tensor(name, shape, dt))

        def sem(name):
            return ctx.enter_context(nc.semaphore(name))

        def scratch(name, *shape):
            return nc.dram_tensor(name, shape, F32, kind="Internal").ap()

        blocks = sum(SEQS) // P
        x1_dram = scratch("x1_scratch", blocks, P, D)
        h2_dram = scratch("h2_scratch", PASSES, P, KC, TOK)
        score_dram = scratch("score_scratch", blocks * HEADS, P, 2 * P)
        gt2_dram = scratch("gt2_scratch", 2, P, D)
        gate_dram = scratch("gate_scratch", PASSES, QUARTERS, P, P, STAGE)

        cst = sb("cst", [P, C_N])
        ident, ones, rot = cst[:, C_ID:C_ID + P], cst[:, C_ONE:C_ONE + P], cst[:, C_ROT:C_ROT + P]
        iota = cst[:, C_IOTA:C_IOTA + P]
        edge = cst[:, C_EDGE:C_EDGE + 64].rearrange("p (g n) -> p g n", g=4)
        mod = sb("mod", [P, 48, 2])
        scl = sb("scl", [P, 2, 2, KC])
        silu_c = sb("silu_c", [P, KC, 2])
        small = sb("small", [P, 16])
        gsub = sb("gsub", [P, 1])
        nlam = sb("nlam", [P, 1])
        hot2 = sb("hot2", [P, 2, 4, P])
        score_in = sb("score_in", [P, 2, P])
        best, besti, bestf = sb("best", [P, 2, TOPK]), sb("besti", [P, 2, TOPK], U32), sb("bestf", [P, 2, TOPK])
        cand = sb("cand", [P, 2, TOPK, TOPK])
        pair = sb("pair", [P, TOPK])
        jbest, jhalf, jf = sb("jbest", [P, TOPK], U32), sb("jhalf", [P, 2, TOPK], U32), sb("jf", [P, 2, TOPK])
        sel = sb("sel", [P, 3, 2 * P])
        gsum = sb("gsum", [P, 16])
        trunk_memory = ExitStack()

        def trunk_sb(name, shape, dt=F32):
            return trunk_memory.enter_context(nc.sbuf_tensor(name, shape, dt))

        ring = trunk_sb("ring", [P, 2 * UNIT])
        arena = trunk_sb("arena", [P, ARENA])
        n_hi, n_lo = trunk_sb("n_hi", [P, KC, SMAX], F32R), trunk_sb("n_lo", [P, KC, SMAX], F32R)
        w_hi, w_lo = trunk_sb("w_hi", [P, 3, TILE], F32R), trunk_sb("w_lo", [P, 3, TILE], F32R)
        par = trunk_sb("par", [P, V_N])

        place = [0]

        def lay(*dims):
            n = int(np.prod(dims))
            a = arena[:, place[0]:place[0] + n]
            place[0] += n
            names = "abcd"[:len(dims)]
            if len(dims) > 1:
                a = a.rearrange("p (%s) -> p %s" % (" ".join(names), " ".join(names)),
                                **{k: v for k, v in zip(names, dims)})
            return a

        hbuf = lay(KC, SMAX)
        obuf = lay(KC, SMAX)
        zbuf = lay(KC, SMAX)
        pbuf = lay(4, LROW)
        ptmp = lay(2, LROW)
        pdif = lay(4, SMAX)
        qkraw = lay(2, SMAX)
        rtmp = lay(SMAX)
        vh = lay(2, SMAX)
        expd = lay(2, 2, SMAX)
        amix = lay(2, SMAX)
        sq = lay(2, SMAX)
        rstd = lay(SMAX)
        ovar = zbuf
        cossin = lay(2, SMAX)
        poolw = lay(4, P)
        assert place[0] <= ARENA, place
        place[0] = 0
        qk = lay(2, 2, SMAX)
        amix_t = lay(4, SMAX)
        spare = (ovar[:, :, SEQS[0]:SEQS[0] + 2 * P], obuf[:, :, SEQS[0]:SEQS[0] + 2 * P])
        base_topk = 2 * KC * SMAX
        place[0] = base_topk
        keybd = lay(HEADS, 2 * P)
        qh = lay(2, SMAX)
        place[0] = base_topk + KC * SMAX
        sc = lay(2, 4 * 2 * P)
        x1tok = lay(2, D)
        gt2row = lay(D)
        diag = lay(KC, P)
        trunk_memory.close()

        raw = sb("raw", [P, 4, 2 * D])
        gate_in = sb("gate_in", [P, 2, QUARTERS, 2, STAGE])
        hot2g = gate_in[:].rearrange("p a q j s -> p a (q j s)").rearrange("p a (x n) -> p a x n", n=P)
        u_hi, u_lo = sb("u_hi", [P, 2, KC, P], F32R), sb("u_lo", [P, 2, KC, P], F32R)
        v_hi, v_lo = sb("v_hi", [P, 2, D], F32R), sb("v_lo", [P, 2, D], F32R)
        h_hi, h_lo = sb("h_hi", [P, KC, TOK], F32R), sb("h_lo", [P, KC, TOK], F32R)
        c_hi, c_lo = sb("c_hi", [P, 2, TOK], F32R), sb("c_lo", [P, 2, TOK], F32R)
        coef = sb("coef", [P, 2, TOK])
        staged = sb("staged", [P, 2, P, STAGE])
        hot1, hot2h, hot2l = (sb(n, [P, 2, 4, P], F32R) for n in ("hot1", "hot2h", "hot2l"))
        sel_t = sb("sel_t", [P, 3, TOK])
        gate_hi = sb("gate_hi", [P, TOK], F32R)
        gate_lo = sel_t[:, 2, :]
        f_gt2, f_gf = sb("f_gt2", [P, D]), sb("f_gf", [P, D])
        f_x1, f_y = sb("f_x1", [P, 2, D]), sb("f_y", [P, 2, D])

        ps = ctx.enter_context(nc.psum_tensor("ps", [P, 8, 512], F32))

        consts_in = sem("consts_in")
        group_in = sem("group_in")
        phase = sem("phase")
        unit_in = [sem("unit_in0"), sem("unit_in1")]
        silu_a, silu_b, ada_in, ada_done, mod_ready = (
            sem("silu_a"), sem("silu_b"), sem("ada_in"), sem("ada_done"), sem("mod_ready"))
        lam_dot, lam_exp = sem("lam_dot"), sem("lam_exp")
        sq_ready, sq_summed, var_ready, rstd_ready, norm_done = (
            sem("sq_ready"), sem("sq_summed"), sem("var_ready"), sem("rstd_ready"), sem("norm_done"))
        scaled, n_rounded, n_split = sem("scaled"), sem("n_rounded"), sem("n_split")
        w_hi_ready, w_lo_ready, gate_done = sem("w_hi_ready"), sem("w_lo_ready"), sem("gate_done")
        p_done, p_copied, pool_diff = sem("p_done"), sem("p_copied"), sem("pool_diff")
        mix_done, mix_copied = sem("mix_done"), sem("mix_copied")
        proj = {k: sem(k + "_proj") for k in "qkv"}
        copied = {k: sem(k + "_copied") for k in "qkv"}
        rotated = {k: sem(k + "_rotated") for k in "qk"}
        roped = {k: sem(k + "_roped") for k in "qk"}
        scored, maxed, expd_ready, mixed, turned, turned_copied = (
            sem("scored"), sem("maxed"), sem("expd_ready"), sem("mixed"), sem("turned"), sem("turned_copied"))
        pv_done, o_copied = sem("pv_done"), sem("o_copied")
        z_done, sig_done, z_ready = sem("z_done"), sem("sig_done"), sem("z_ready")
        out_done, x1_ready, x_again = sem("out_done"), sem("x1_ready"), sem("x_again")
        x1_turned, x1_copied, x1_stored = sem("x1_turned"), sem("x1_copied"), [sem("x1_stored0"), sem("x1_stored1")]
        keys_in, pq_done, pq_copied, keyed, keyed_copied = (
            sem("keys_in"), sem("pq_done"), sem("pq_copied"), sem("keyed"), sem("keyed_copied"))
        scores_stored = [sem("scores_stored0"), sem("scores_stored1")]
        h2_stored = sem("h2_stored")
        o_squared, o_summed, o_var, o_rstd, o_normed = (
            sem("o_squared"), sem("o_summed"), sem("o_var"), sem("o_rstd"), sem("o_normed"))
        diag_ready, gt2_done, gt2_copied, gt2_stored = (
            sem("diag_ready"), sem("gt2_done"), sem("gt2_copied"), sem("gt2_stored"))
        score_loaded, score_free = [sem("score_loaded%d" % i) for i in range(PASSES)], sem("score_free")
        shifted, exped, sel_ready, sel_turned, sel_copied = (
            sem("shifted"), sem("exped"), sem("sel_ready"), sem("sel_turned"), sem("sel_copied"))
        hot2_ready, hot2h_ready, hot2l_ready = (
            sem("hot2_ready"), sem("hot2h_ready"), sem("hot2l_ready"))
        g_done, g_copied = sem("g_done"), sem("g_copied")
        gates_early = sem("gates_early")
        gates_stored = [sem("gates_stored0"), sem("gates_stored1")]
        raw_in = [sem("raw_in%d" % i) for i in range(4)]
        gate_loaded = [sem("gate_loaded%d" % i) for i in range(2)]
        STEPS = TOK // 4
        h_in, h_hi_ready, h_lo_ready = sem("h_in"), sem("h_hi_ready"), sem("h_lo_ready")
        u_hi_ready, u_lo_ready, v_hi_ready, v_lo_ready = (
            sem("u_hi_ready"), sem("u_lo_ready"), sem("v_hi_ready"), sem("v_lo_ready"))
        s_done, gelu_done, coef_ready, c_hi_ready, c_lo_ready, v_done = (
            sem("s_done"), sem("gelu_done"), sem("coef_ready"), sem("c_hi_ready"), sem("c_lo_ready"), sem("v_done"))
        fin_in, acc_read, y_ready, y_squared, y_var, y_rstd, y_final, y_stored = (
            sem("fin_in"), sem("acc_read"), sem("y_ready"), sem("y_squared"), sem("y_var"), sem("y_rstd"),
            sem("y_final"), sem("y_stored"))

        block = ctx.enter_context(nc.Block())

        phases = {}

        def all_done(eng):
            n = phases[id(eng)] = phases.get(id(eng), 0) + 1
            eng.drain()
            eng.sem_inc(phase, 1)
            eng.wait_ge(phase, 5 * n)

        def wtile(u, i):
            o = (u % 2) * UNIT + i * TILE
            return ring[:, o:o + TILE].rearrange("p (k n) -> p k n", k=KC)

        def unit_landed(eng, u):
            eng.wait_ge(unit_in[u % 2], 16 * (u // 2 + 1))

        def load_scores(eng, nxt, i):
            u = i + 16 * nxt
            after(eng, score_free, u)
            eng.dma_start(score_in[:].rearrange("p a n -> p (a n)"),
                          score_dram[bass.ds(u, 1)].rearrange("a p n -> (a p) n")).then_inc(score_loaded[nxt], 16)

        zbanks = ((0, 2, 1, 3), (7, 4, 5, 6))
        ubase = [ADA_FIRST + g * UNITS_GROUP for g in range(2)]
        qbase = [0, HEADS * SEQS[0] // P]
        group_of = (0, 1, 1)
        tbase = [0, SEQS[0] // P]

        @block.sync
        def _(sp):
            sp.dma_start(par[:], params).then_inc(consts_in, 16)
            sp.dma_start(cst[:], consts).then_inc(consts_in, 16)

            def load_unit(u, half):
                sp.dma_start(ring[:, half * UNIT:(half + 1) * UNIT], u).then_inc(unit_in[half], 16)

            def weight_unit(u):
                return weights[bass.ds(u, 1)].rearrange("a p n -> (a p) n")

            for u in range(2):
                load_unit(weights[u], u)
            for g, S in enumerate(SEQS):
                if g:
                    all_done(sp)
                if g == 0:
                    sp.dma_start(hbuf[:, :, 0:S], x_t[g]).then_inc(group_in, 16)
                    for u in range(2, ADA_FIRST):
                        sp.wait_ge(ada_done, u - 1)
                        load_unit(weights[u], u % 2)
                sp.dma_start(cossin[:, :, 0:S], rope[:, :, 0:S]).then_inc(group_in, 16)
                sp.dma_start(poolw, pool_w).then_inc(group_in, 16)
                b = ubase[g]

                def load(n, used, count):
                    sp.wait_ge(used, count)
                    load_unit(weights[UNITS_ADA + n], (b + n) % 2)

                load(0, ada_done, ADA_FIRST - 1)
                load(1, ada_done, ADA_FIRST)
                load(2, p_done, 4 * g + 4)
                with sp.Fori(1, HEADS // 2) as i:
                    for j in range(2):
                        sp.wait_ge(proj["v"], 2 * i + (8 * g + j - 1))
                        load_unit(weight_unit(2 * i + (UNITS_ADA + 1 + j)), (b + 1 + j) % 2)
                load(9, proj["v"], 8 * g + 7)
                load(10, proj["v"], 8 * g + 8)
                with sp.Fori(1, KC // 2) as i:
                    for j in range(2):
                        sp.wait_ge(z_done, 2 * i + (8 * g + j - 1))
                        load_unit(weight_unit(2 * i + (UNITS_ADA + 9 + j)), (b + 9 + j) % 2)
                load(17, z_done, 8 * g + 7)
                load(18, z_done, 8 * g + 8)
                sp.wait_ge(z_done, HEADS * (g + 1))
                sp.dma_start(obuf[:, :, 0:S], x_t[g]).then_inc(x_again, 16)
                load(19, out_done, 8 * g + 4)
                load(20, out_done, 8 * g + 8)
                sp.dma_start(keybd, keys).then_inc(keys_in, 16)
                for tb in range(S // P):
                    sp.wait_ge(x1_copied, tbase[g] + tb + 1)
                    sp.dma_start(x1_dram[tbase[g] + tb], x1tok[:, tb % 2, :]).then_inc(x1_stored[tb % 2], 16)
                sp.wait_ge(norm_done, KC * (g + 1))
                for n in range(S // TOK):
                    sp.dma_start(h2_dram[g + n], obuf[:, :, n * TOK:(n + 1) * TOK]).then_inc(h2_stored, 16)
                if g + 1 < len(SEQS):
                    sp.wait_ge(x1_copied, tbase[g] + S // P)
                    sp.dma_start(hbuf[:, :, 0:SEQS[g + 1]], x_t[g + 1]).then_inc(group_in, 16)
                sp.wait_ge(gt2_copied, g + 1)
                sp.dma_start(gt2_dram[g], gt2row).then_inc(gt2_stored, 16)
                for h in range(HEADS):
                    sp.wait_ge(keyed_copied, 8 * g + h + 1)
                    dst = score_dram.rearrange("(t h) p n -> h p t n", h=HEADS)[h, :, tbase[g]:tbase[g] + S // P, :]
                    sp.dma_start(dst, sc[:, h % 2, 0:2 * S].rearrange("p (t n) -> p t n", n=2 * P)
                                 ).then_inc(scores_stored[h % 2], 16)
                for j in range(2):
                    sp.wait_ge(x1_stored[j], 16 * (tbase[g] + S // P) // 2)
                    sp.wait_ge(scores_stored[j], 64 * (g + 1))
                sp.wait_ge(h2_stored, 16 * (g + S // TOK))
                sp.wait_ge(gt2_stored, 16 * (g + 1))

            all_done(sp)
            sp.dma_start(f_gf[:], g_final).then_inc(fin_in, 16)
            sp.dma_start(f_y[:].rearrange("p a n -> p (a n)"),
                         h2_dram[0].rearrange("p k t -> p (k t)")).then_inc(h_in, 16)

            def load_tile(n, i, t):
                k = 4 * i + (t + P * n)
                after(sp, u_lo_ready, k - 3)
                after(sp, v_lo_ready, k - 3)
                sp.dma_start(raw[:, t, :], table[bass.ds(4 * i + t, 1)].rearrange("a p n -> (a p) n")
                             ).then_inc(raw_in[t], 16)

            def load_gates(n, i, pair):
                k = 4 * i + (2 * pair + P * n)
                after(sp, coef_ready, k - 2)
                src = gate_dram[n, :, :, bass.ds(4 * i + 2 * pair, 2), :].rearrange("q p j s -> p q (j s)")
                sp.dma_start(gate_in[:, pair].rearrange("p q j s -> p q (j s)"), src).then_inc(gate_loaded[pair], 16)

            def store_y(n):
                for j in range(2):
                    sp.wait_ge(y_final, 2 * n + j + 1)
                    r = (n - group_of[n]) * TOK + j * P
                    sp.dma_start(outs[group_of[n]][0, r:r + P, :], f_y[:, j, :]).then_inc(y_stored, 16)
                sp.wait_ge(y_stored, 32 * (n + 1))

            for n in range(PASSES):
                nxt = n + 1 if n + 1 < PASSES else None

                def body(i, searching):
                    for t in range(4):
                        if searching and t == 2:
                            load_scores(sp, nxt, i)
                        load_tile(n, i, t)
                        if t % 2 == 0:
                            load_gates(n, i, t // 2)

                for t in range(4):
                    load_tile(n, 0, t)
                sp.wait_ge(gates_stored[0], 32 * (n + 1))
                sp.wait_ge(gates_stored[1], 32 * n + 16)
                sp.wait_ge(gates_early, 16 * (n + 1))
                for pair in range(2):
                    load_gates(n, 0, pair)
                if nxt is not None:
                    load_scores(sp, nxt, 0)
                body(1, nxt is not None)
                sp.wait_ge(gates_stored[1], 32 * (n + 1))
                if n:
                    store_y(n - 1)
                sp.dma_start(f_gt2[:], gt2_dram[group_of[n]]).then_inc(fin_in, 16)
                for j in range(2):
                    sp.dma_start(f_x1[:, j, :], x1_dram[2 * n + j]).then_inc(fin_in, 16)
                if nxt is not None:
                    if n == 0:
                        sp.wait_ge(h_lo_ready, 1)
                    sp.dma_start(f_y[:].rearrange("p a n -> p (a n)"),
                                 h2_dram[nxt].rearrange("p k t -> p (k t)")).then_inc(h_in, 16)
                    with sp.Fori(2, 16) as i:
                        body(i, True)
                    with sp.Fori(16, 32) as i:
                        body(i, False)
                else:
                    with sp.Fori(2, 32) as i:
                        body(i, False)
            store_y(PASSES - 1)

        @block.tensor
        def _(pe):
            mm = nc.tensor.matmul
            pe.wait_ge(consts_in, 32)
            pe.wait_ge(silu_b, 1)

            def modulation(bank, u, tile):
                for i in range(4):
                    for k in range(KC):
                        last = mm(ps[:, bank, bass.ds(8 * u + 2 * i, 2)], tile(i)[:, k, :], silu_c[:, k, :],
                                  start=(k == 0), stop=(k == KC - 1))
                last.then_inc(ada_done, 1)

            for u in range(ADA_FIRST):
                unit_landed(pe, u)
                modulation(0, u, lambda i: wtile(u, i))

            for g, S in enumerate(SEQS):
                B = S // P
                b = ubase[g]
                if g:
                    all_done(pe)

                def sum_squares(n0):
                    for c in range(KC):
                        pe.wait_ge(sq_ready, n0 + c + 1)
                        mm(ps[:, 2, 0:S], ones, sq[:, c % 2, 0:S], start=(c == 0),
                           stop=(c == KC - 1)).then_inc(sq_summed, 1)

                def product(bank, w, src, n=KC, normed=False):
                    for k in range(n):
                        if normed:
                            pe.wait_ge(norm_done, KC * g + k + 1)
                        last = mm(ps[:, bank, 0:S], w[:, k, :], src[:, k, 0:S], start=(k == 0), stop=(k == n - 1))
                    return last

                def split_product(bank, tile, k0=0, k1=KC, normed=False):
                    n, j = tile
                    if k0 == 0:
                        pe.wait_ge(w_lo_ready, n + (SPLIT_TILES * g + 1))
                    for k in range(k0, k1):
                        if normed:
                            pe.wait_ge(n_split, KC * g + k + 1)
                        wh, wl = (w[:, j, k * P:(k + 1) * P] for w in (w_hi, w_lo))
                        xh, xl = n_hi[:, k, 0:S], n_lo[:, k, 0:S]
                        for x, (a, c) in enumerate(((wh, xh), (wh, xl), (wl, xh))):
                            last = mm(ps[:, bank, 0:S], a, c, start=k == 0 and x == 0,
                                      stop=k == KC - 1 and x == 2, skip_group_check=True)
                    return last

                def gate_tile(c, m):
                    return 4 + 3 * HEADS + 2 * c + m, 2 if isinstance(c, int) and (c, m) == (1, 0) else m

                nsq = 2 * KC * g
                pe.wait_ge(group_in, 48 * (g + 1))
                sum_squares(nsq)

                for c in range(4):
                    n = 4 * g + c
                    if c >= 2:
                        pe.wait_ge(p_copied, n - 1)
                    split_product(c % 2, (c, 1 + c % 2), normed=c == 0).then_inc(p_done, 1)
                pe.wait_ge(p_copied, 4 * g + 4)

                def mix_groups(c):
                    n = 4 * g + c
                    pe.wait_ge(pool_diff, n + 1)
                    if c:
                        pe.wait_ge(mix_copied, n)
                    mm(ps[:, 7, 0:S], poolw[:, c, :], pdif[:, c, 0:S], start=True, stop=True).then_inc(mix_done, 1)

                def sum_head(m):
                    pe.wait_ge(o_squared, m + 1)
                    after(pe, o_var, m)
                    mm(ps[:, 6, 0:S], ones, sq[:, 0, 0:S], start=True, stop=True).then_inc(o_summed, 1)

                def head(h, par_, do_proj, do_att):
                    hg = 8 * g + h
                    q0 = qbase[g] + (h - 1) * B

                    def scores(j):
                        if j == 0:
                            for x in "qk":
                                after(pe, roped[x], hg)
                        after(pe, expd_ready, q0 + j)
                        o = 1 - par_
                        for m in range(2):
                            r = slice(HALF * m, HALF * m + HALF)
                            last = mm(ps[:, 3 + m, 0:S], qk[r, o, 0, j * P:(j + 1) * P], qk[r, o, 1, 0:S],
                                      start=True, stop=True)
                        last.then_inc(scored, 1)

                    def turn(j):
                        pe.wait_ge(mixed, q0 + j + 1)
                        after(pe, turned_copied, q0 + j)
                        for kb in range(B):
                            last = nc.tensor.transpose(ps[:, 5, kb * P:(kb + 1) * P],
                                                       amix[:, j % 2, kb * P:(kb + 1) * P], ident)
                        last.then_inc(turned, 1)

                    def project(x, i, bank, free_sem=None, free_n=0, part=(0, 1)):
                        after(pe, free_sem, free_n)
                        n, j = 3 * h + (4 + i), i
                        if x != "v":
                            last = split_product(bank, (n, j), int(part[0] * KC), int(part[1] * KC))
                        else:
                            if part[0] == 0:
                                pe.wait_ge(w_lo_ready, n + (SPLIT_TILES * g + 1))
                            for t in range(int(part[0] * B), int(part[1] * B)):
                                for k in range(KC):
                                    wh, wl = (w[:, j, k * P:(k + 1) * P] for w in (w_hi, w_lo))
                                    xh, xl = (y[:, k, t * P:(t + 1) * P] for y in (n_hi, n_lo))
                                    for y, (a, c) in enumerate(((xh, wh), (xh, wl), (xl, wh))):
                                        last = mm(ps[:, bank, t * P:(t + 1) * P], a, c, start=k == 0 and y == 0,
                                                  stop=k == KC - 1 and y == 2, skip_group_check=True)
                        if part[1] == 1:
                            last.then_inc(proj[x], 1)

                    def gate_part(j, m, part):
                        last = split_product(zbanks[j][m], gate_tile(j, m), *part)
                        if part[1] == KC:
                            last.then_inc(gate_done, 1)

                    def rotate(x, i):
                        pe.wait_ge(copied[x], hg + 1)
                        if x == "k":
                            pe.wait_ge(roped["q"], hg + 1)
                        else:
                            after(pe, roped["k"], hg)
                        mm(ps[:, 2, 0:S], rot, qkraw[:, i, 0:S], start=True, stop=True).then_inc(rotated[x], 1)

                    if do_att:
                        scores(0)
                    if do_proj:
                        project("q", 0, 0, copied["v"], hg, part=(0, 0.75))
                    else:
                        if g == 0:
                            pe.wait_ge(mod_ready, 2)
                        mix_groups(0)
                        pe.wait_ge(copied["v"], 8 * g + HEADS)
                        gate_part(0, 0, (0, 4))
                        mix_groups(1)
                        gate_part(0, 0, (4, 8))
                    if do_att:
                        if not isinstance(h, int) or h >= 2:
                            sum_head(hg - 2)
                        scores(1)
                        turn(0)
                    if do_proj:
                        project("q", 0, 0, part=(0.75, 1))
                        project("k", 1, 1, o_copied, hg - 1, part=(0, 0.5))
                    else:
                        mix_groups(2)
                        pe.wait_ge(roped["k"], 8 * g + HEADS)
                        gate_part(0, 1, (0, 4))
                        mix_groups(3)
                        gate_part(0, 1, (4, 8))
                    if do_att:
                        if B > 2:
                            scores(2)
                        turn(1)
                    if do_proj:
                        rotate("q", 0)
                        project("k", 1, 1, part=(0.5, 1))
                        project("v", 2, 0, copied["q"], hg + 1, part=(0, 1 / B))
                    else:
                        pe.wait_ge(mix_copied, 4 * g + 4)
                        gate_part(1, 0, (0, 8))
                    if do_att and B > 2:
                        scores(3)
                        turn(2)
                    if do_proj:
                        rotate("k", 1)
                        if B > 2:
                            project("v", 2, 0, part=(1 / B, 3 / B))
                    if do_att and B > 2:
                        turn(3)
                    if do_proj:
                        project("v", 2, 0, part=(1 - 1 / B, 1))
                    if do_att:
                        pe.wait_ge(turned_copied, q0 + B)
                        pe.wait_ge(copied["v"], hg)
                        if do_proj:
                            pe.wait_ge(copied["k"], hg + 1)
                        for kb in range(B):
                            last = mm(ps[:, 1, 0:S], vh[:, 1 - par_, kb * P:(kb + 1) * P],
                                      amix_t[:, kb, 0:S], start=(kb == 0), stop=(kb == B - 1))
                        last.then_inc(pv_done, 1)
                    if do_proj and g == 0:
                        pe.wait_ge(ada_in, 64 * h + 64)
                        modulation(7, ADA_FIRST + h, lambda i: spare[i // 2][:, :, (i % 2) * P:(i % 2 + 1) * P])

                head(0, 0, True, False)
                head(1, 1, True, True)
                with pe.Fori(0, HEADS // 2 - 1) as i:
                    head(2 * i + 2, 0, True, True)
                    head(2 * i + 3, 1, True, True)
                head(HEADS, 0, False, True)

                sum_head(8 * g + HEADS - 1)
                def z_product(j, m):
                    return product(zbanks[j][m], wtile(b + 9 + j, m), (obuf, pdif)[m - 2], 4 if m == 3 else KC)

                unit_landed(pe, b + 9)
                z_product(0, 3)
                split_product(zbanks[1][1], gate_tile(1, 1)).then_inc(gate_done, 1)
                unit_landed(pe, b + 10)
                pe.wait_ge(o_var, 8 * g + 8)
                z_product(1, 3)
                pe.wait_ge(o_normed, 8 * g + 8)
                for j in range(2):
                    z_product(j, 2).then_inc(z_done, 1)
                with pe.Fori(1, KC // 2) as i:
                    for j in range(2):
                        c = 2 * i + j
                        pe.wait_ge(unit_in[(b + 9 + j) % 2], 16 * i + 16 * ((b + 9 + j) // 2 + 1))
                        pe.wait_ge(z_ready, c + (8 * g - 1))
                        for m in range(2):
                            split_product(zbanks[j][m], gate_tile(c, m)).then_inc(gate_done, 1)
                        z_product(j, 2)
                        z_product(j, 3).then_inc(z_done, 1)
                pe.wait_ge(z_ready, 8 * g + 8)

                for c in range(KC):
                    u = b + 17 + c // 4
                    if c % 4 == 0:
                        unit_landed(pe, u)
                    if c >= 2:
                        pe.wait_ge(x1_ready, 8 * g + c - 1)
                    product(c % 2, wtile(u, c % 4), zbuf).then_inc(out_done, 1)
                pe.wait_ge(x1_ready, 8 * g + 8)
                sum_squares(nsq + KC)
                for t in range(B):
                    after(pe, x1_copied, tbase[g] + t)
                    for k in range(KC):
                        last = nc.tensor.transpose(ps[:, 6 + k // 4, (k % 4) * P:(k % 4 + 1) * P],
                                                   hbuf[:, k, t * P:(t + 1) * P], ident)
                    last.then_inc(x1_turned, 1)
                pe.wait_ge(diag_ready, g + 1)
                pe.wait_ge(x1_copied, tbase[g] + B)
                for k in range(KC):
                    last = mm(ps[:, 6 + k // 4, (k % 4) * P:(k % 4 + 1) * P], ones, diag[:, k, :],
                              start=True, stop=True)
                last.then_inc(gt2_done, 1)

                pe.wait_ge(keys_in, 16 * (g + 1))

                def key_scores(h):
                    n = 8 * g + h
                    pe.wait_ge(pq_copied, n + 1)
                    if h >= 2:
                        pe.wait_ge(keyed_copied, n - 1)
                    for t in range(B):
                        bank = 2 + 2 * (h % 2) + t // 2
                        o = (t % 2) * 2 * P
                        last = mm(ps[:, bank, o:o + 2 * P], qh[:, h % 2, t * P:(t + 1) * P], keybd[:, h, :],
                                  start=True, stop=True)
                    last.then_inc(keyed, 1)

                for h in range(HEADS):
                    u = b + 19 + h // 4
                    if h % 4 == 0:
                        unit_landed(pe, u)
                    if h >= 2:
                        pe.wait_ge(pq_copied, 8 * g + h - 1)
                    product(h % 2, wtile(u, h % 4), obuf, normed=h == 0).then_inc(pq_done, 1)
                    if h:
                        key_scores(h - 1)
                key_scores(HEADS - 1)

            all_done(pe)

            def products(out, pairs, start, stop):
                for x, (a, b_) in enumerate(pairs):
                    last = mm(out, a, b_, start=start and x == 0, stop=stop and x == len(pairs) - 1,
                              skip_group_check=True)
                return last

            def score(k, t):
                pe.wait_ge(u_lo_ready, k + 1)
                after(pe, gelu_done, k - 1)
                pairs = []
                for c in range(KC):
                    uh, ul = u_hi[:, t % 2, c, :], u_lo[:, t % 2, c, :]
                    pairs += [(uh, h_hi[:, c, :]), (uh, h_lo[:, c, :]), (ul, h_hi[:, c, :])]
                products(ps[:, t % 2, 0:TOK], pairs, True, True).then_inc(s_done, 1)

            def combine(k, t, start=False, stop=False):
                pe.wait_ge(v_lo_ready, k + 1)
                pe.wait_ge(c_lo_ready, k + 1)
                j = t % 2
                for tb in range(2):
                    ch, cl = c_hi[:, j, tb * P:(tb + 1) * P], c_lo[:, j, tb * P:(tb + 1) * P]
                    for f in range(2):
                        vh_, vl = v_hi[:, j, f * 512:(f + 1) * 512], v_lo[:, j, f * 512:(f + 1) * 512]
                        last = products(ps[:, 4 + 2 * tb + f, :], [(ch, vh_), (ch, vl), (cl, vh_)], start, stop)
                last.then_inc(v_done, 1)

            def gate_step(s, t, whole):
                pe.wait_ge(hot2h_ready, s + 1)
                pe.wait_ge(hot2l_ready, s + 1)
                after(pe, g_copied, s - 1)
                j = t % 2
                for x in range(4):
                    if whole:
                        last = mm(ps[:, 2 + j, x * P:(x + 1) * P], hot1[:, j, x, :].bitcast(F32),
                                  hot2g[:, j, x, :], start=True, stop=True)
                        continue
                    last = products(ps[:, 2 + j, x * P:(x + 1) * P],
                                    [(hot1[:, j, x, :], hot2h[:, j, x, :]), (hot1[:, j, x, :], hot2l[:, j, x, :])],
                                    True, True)
                last.then_inc(g_done, 1)

            for n in range(-1, PASSES):
                nxt = n + 1 if n + 1 < PASSES else None

                def body(i, building=False, first=False):
                    for t in range(4):
                        k = 4 * i + (t + P * n)
                        if n >= 0:
                            score(k, t)
                        if n >= 0 and not (first and t == 0):
                            if first and t == 1:
                                after(pe, acc_read, n)
                            combine(k - 1, t + 3, start=first and t == 1)
                        if building:
                            gate_step(4 * i + (STEPS * (nxt - 1) + t), t, whole=n < 0)

                if n >= 0:
                    pe.wait_ge(h_lo_ready, n + 1)
                    body(0, first=True)
                    with pe.Fori(1, 16) as i:
                        body(i)
                if nxt is not None:
                    pe.wait_ge(sel_ready, nxt + 1)
                    after(pe, g_copied, STEPS * nxt)
                    for tb in range(2):
                        for x in range(3):
                            last = nc.tensor.transpose(ps[:, 2 + tb, x * P:(x + 1) * P],
                                                       sel[:, x, tb * P:(tb + 1) * P], ident)
                    last.then_inc(sel_turned, 1)
                    pe.wait_ge(sel_copied, nxt + 1)
                    body(16, building=True)
                    with pe.Fori(17, 32) as i:
                        body(i, building=True)
                else:
                    with pe.Fori(16, 32) as i:
                        body(i)
                if n >= 0:
                    combine(P * (n + 1) - 1, 3, stop=True)

        @block.scalar
        def _(act):
            A = nc.scalar.activation
            act.wait_ge(consts_in, 32)
            cs = par[:, V_C:V_C + 16].rearrange("p (k g) -> p k g", g=2)
            A(silu_c[:], cs, ACT.Sigmoid).then_inc(silu_a, 1)
            act.wait_ge(lam_dot, 1)
            A(small[:, 2:4], small[:, 0:2], ACT.Exp).then_inc(lam_exp, 1)

            for g, S in enumerate(SEQS):
                B = S // P
                if g:
                    all_done(act)
                nsq = 2 * KC * g

                def squares(n0):
                    for c in range(KC):
                        if c >= 2:
                            act.wait_ge(sq_summed, n0 + c - 1)
                        A(sq[:, c % 2, 0:S], hbuf[:, c, 0:S], ACT.Square).then_inc(sq_ready, 1)

                act.wait_ge(group_in, 48 * (g + 1))
                squares(nsq)
                b = ubase[g]
                for c in range(2):
                    act.wait_ge(unit_in[b % 2], 16 * (b // 2 + 1))
                    nc.scalar.copy(w_hi[:, 1 + c, :], ring[:, (b % 2) * UNIT + c * TILE:(b % 2) * UNIT + (c + 1) * TILE]
                                   ).then_inc(w_hi_ready, 1)
                act.wait_ge(var_ready, 2 * g + 1)
                A(rstd[:, 0:S], rstd[:, 0:S], ACT.Sqrt).then_inc(rstd_ready, 1)

                def shift(n, dst, c):
                    act.wait_ge(scaled, KC * (2 * g + n) + c + 1)
                    src = dst if n else hbuf
                    A(dst[:, c, 0:S], src[:, c, 0:S], ACT.Identity, bias=mod[:, 24 * n + c, g:g + 1]
                      ).then_inc(norm_done if n else n_rounded, 1)

                def split_weights(j, u, i, later=0):
                    act.wait_ge(unit_in[u % 2], 16 * later + 16 * (u // 2 + 1))
                    o = (u % 2) * UNIT + i * TILE
                    nc.scalar.copy(w_hi[:, j, :], ring[:, o:o + TILE]).then_inc(w_hi_ready, 1)

                for c in range(KC):
                    shift(0, n_hi, c)
                for c in range(4):
                    act.wait_ge(p_done, 4 * g + c + 1)
                    nc.scalar.copy(pbuf[:, c, PAD:PAD + S], ps[:, c % 2, 0:S]).then_inc(p_copied, 1)
                    if c < 2:
                        split_weights(1 + c, b, c + 2)
                    if c:
                        split_weights(c - 1, b + 1, c - 1)

                def root_variance(x):
                    half = ovar[:, x * HEADS // 2:(x + 1) * HEADS // 2, 0:S]
                    act.wait_ge(o_var, 8 * g + (x + 1) * HEADS // 2)
                    A(half, half, ACT.Sqrt).then_inc(o_rstd, 1)

                def head(h, par_, do_proj, do_att):
                    hg = 8 * g + h
                    q0 = qbase[g] + (h - 1) * B

                    def expo(j):
                        pe_ = j % 2
                        act.wait_ge(maxed, q0 + j + 1)
                        after(act, mixed, q0 + j - 1)
                        for m in range(2):
                            last = A(expd[:, pe_, m, 0:S], ps[:, 3 + m, 0:S], ACT.Exp,
                                     bias=small[:, 4 + 2 * pe_ + m:5 + 2 * pe_ + m], scale=HALF ** -0.5,
                                     accum_out=small[:, 8 + 2 * pe_ + m:9 + 2 * pe_ + m])
                        last.then_inc(expd_ready, 1)

                    def turned_out(j):
                        act.wait_ge(turned, q0 + j + 1)
                        if j == 0:
                            after(act, pv_done, hg - 1)
                        nc.scalar.copy(amix_t[:, 0:B, j * P:(j + 1) * P],
                                       ps[:, 5, 0:S].rearrange("p (b n) -> p b n", n=P)).then_inc(turned_copied, 1)

                    def raw_out(x, i, bank):
                        act.wait_ge(proj[x], hg + 1)
                        if x == "v":
                            after(act, pv_done, hg - 1)
                            nc.scalar.copy(vh[:, par_, 0:S], ps[:, bank, 0:S]).then_inc(copied[x], 1)
                        else:
                            after(act, roped[x], hg)
                            nc.scalar.copy(qkraw[:, i, 0:S], ps[:, bank, 0:S]).then_inc(copied[x], 1)

                    def mix_out(c):
                        act.wait_ge(mix_done, 4 * g + c + 1)
                        A(pdif[:, c, 0:S], ps[:, 7, 0:S], ACT.Copy,
                          scale=par[:, V_PSC + c:V_PSC + c + 1]).then_inc(mix_copied, 1)

                    def split_next(h, par_, i):
                        split_weights(i, b + 1 + par_, i, later=(h - par_) // 2)

                    if do_proj and g == 0:
                        after(act, ada_done, h + ADA_FIRST)
                        src = weights[bass.ds(ADA_FIRST + h, 1)].rearrange("a p (x i k n) -> x (a p) i k n",
                                                                           x=2, i=2, k=KC)
                        for x in range(2):
                            for i in range(2):
                                act.dma_start(spare[x][:, :, i * P:(i + 1) * P], src[x, :, i]).then_inc(ada_in, 16)
                    if not do_proj:
                        split_weights(2, b + 10, 0)
                    elif do_att:
                        split_next(h, par_, 2)
                    if do_att:
                        expo(0)
                        if not do_proj:
                            mix_out(0)
                            mix_out(1)
                        turned_out(0)
                        expo(1)
                    if do_proj:
                        raw_out("q", 0, 0)
                        split_next(h + 1, 1 - par_, 0)
                    else:
                        mix_out(2)
                        mix_out(3)
                    if do_att:
                        turned_out(1)
                        if B > 2:
                            expo(2)
                    if do_proj:
                        raw_out("k", 1, 1)
                        split_next(h + 1, 1 - par_, 1)
                    else:
                        act.wait_ge(gate_done, 2 * KC * g + 2)
                        split_weights(1, b + 10, 1)
                    if do_att:
                        for j in range(2, B):
                            turned_out(j)
                            if j + 1 < B:
                                expo(j + 1)
                    if do_proj:
                        raw_out("v", 2, 0)
                    else:
                        root_variance(0)
                    if do_att:
                        act.wait_ge(pv_done, hg)
                        after(act, o_summed, hg - 1)
                        A(sq[:, 0, 0:S], ps[:, 1, 0:S], ACT.Square).then_inc(o_squared, 1)
                        hh = h - 1
                        dst = (obuf[:, hh, 0:S] if isinstance(hh, int)
                               else obuf[:, bass.ds(hh, 1), 0:S].rearrange("p a s -> p (a s)"))
                        nc.scalar.copy(dst, ps[:, 1, 0:S]).then_inc(o_copied, 1)

                head(0, 0, True, False)
                head(1, 1, True, True)
                with act.Fori(0, HEADS // 2 - 1) as i:
                    head(2 * i + 2, 0, True, True)
                    head(2 * i + 3, 1, True, True)
                head(HEADS, 0, False, True)
                root_variance(1)

                def gate_weights(c):
                    for m in range(2):
                        act.wait_ge(gate_done, 2 * KC * g + 2 * c + m - 1)
                        split_weights(m, b + 9 + c, m)

                gate_weights(2)
                for c in range(KC):
                    act.wait_ge(z_done, 8 * g + c + 1)
                    if c >= 2:
                        act.wait_ge(z_ready, 8 * g + c - 1)
                    for m in range(2):
                        last = A(expd[:, c % 2, m, 0:S], ps[:, zbanks[c % 2][m], 0:S], ACT.Sigmoid,
                                 bias=par[:, V_BGATE + 8 * m + c:V_BGATE + 8 * m + c + 1])
                    last.then_inc(sig_done, 1)
                    if 3 <= c + 2 < KC:
                        gate_weights(c + 2)
                act.wait_ge(x1_ready, 8 * g + 8)
                squares(nsq + KC)

                def x1_out(t):
                    act.wait_ge(x1_turned, tbase[g] + t + 1)
                    if t >= 2:
                        act.wait_ge(x1_stored[t % 2], 16 * ((tbase[g] + t) // 2))
                    nc.scalar.copy(x1tok[:, t % 2, :].rearrange("p (a n) -> p a n", a=2),
                                   ps[:, 6:8, :]).then_inc(x1_copied, 1)

                act.wait_ge(var_ready, 2 * g + 2)
                A(rstd[:, 0:S], rstd[:, 0:S], ACT.Sqrt).then_inc(rstd_ready, 1)
                for c in range(KC):
                    if c % 2 == 0 and c // 2 < B:
                        x1_out(c // 2)
                    shift(1, obuf, c)
                act.wait_ge(gt2_done, g + 1)
                nc.scalar.copy(gt2row.rearrange("p (a n) -> p a n", a=2), ps[:, 6:8, :]).then_inc(gt2_copied, 1)
                for h in range(HEADS + 1):
                    if h < HEADS:
                        act.wait_ge(pq_done, 8 * g + h + 1)
                        if h >= 2:
                            act.wait_ge(keyed, 8 * g + h - 1)
                        nc.scalar.copy(qh[:, h % 2, 0:S], ps[:, h % 2, 0:S]).then_inc(pq_copied, 1)
                    if h:
                        m = h - 1
                        act.wait_ge(keyed, 8 * g + h)
                        if m >= 2:
                            act.wait_ge(scores_stored[m % 2], 16 * (4 * g + m // 2))
                        bank = 2 + 2 * (m % 2)
                        nc.scalar.copy(sc[:, m % 2, 0:2 * S].rearrange("p (a n) -> p a n", n=512),
                                       ps[:, bank:bank + S // 256, :]).then_inc(keyed_copied, 1)

            all_done(act)
            copy = nc.scalar.copy

            def flat(t):
                return t.rearrange("p a b -> p (a b)")

            def split_u(k, i, n, t):
                act.wait_ge(raw_in[t % 4], 16 * i + (16 * (P // 4) * n + 16 * (t // 4 + 1)))
                after(act, s_done, k - 1)
                copy(flat(u_hi[:, t % 2]), raw[:, t % 4, 0:D]).then_inc(u_hi_ready, 1)

            def split_v(k, t):
                after(act, v_done, k - 1)
                copy(v_hi[:, t % 2, :], raw[:, t, D:2 * D]).then_inc(v_hi_ready, 1)

            def gelu(k, t):
                act.wait_ge(s_done, k + 1)
                after(act, c_lo_ready, k - 1)
                A(coef[:, t % 2, :], ps[:, t % 2, 0:TOK], ACT.Gelu).then_inc(gelu_done, 1)

            def split_coef(k, t):
                act.wait_ge(coef_ready, k + 1)
                after(act, v_done, k - 1)
                copy(c_hi[:, t % 2, :], coef[:, t % 2, :]).then_inc(c_hi_ready, 1)

            def norm_y(n, part):
                if part == 1:
                    act.wait_ge(y_ready, n + 1)
                    for j in range(2):
                        last = A(f_x1[:, j, :], f_y[:, j, :], ACT.Square, accum_out=small[:, 12 + j:13 + j])
                    last.then_inc(y_squared, 1)
                elif part == 2:
                    act.wait_ge(y_var, n + 1)
                    A(small[:, 14:16], small[:, 14:16], ACT.Sqrt).then_inc(y_rstd, 1)

            for n in range(-1, PASSES):
                nxt = n + 1 if n + 1 < PASSES else None

                def copy_gates(i, q, t):
                    act.wait_ge(g_done, 4 * i + (STEPS * (nxt - 1) + t + 1))
                    col = 16 * i + (4 * t - 16 * (16 + 4 * q))
                    copy(staged[:, q % 2, :, bass.ds(col, 4)],
                         ps[:, 2 + t % 2, :].rearrange("p (t k) -> p k t", t=4)).then_inc(g_copied, 1)

                def flush(q):
                    act.wait_ge(g_copied, 16 * (4 * nxt + q + 1))
                    src = staged[:, q % 2]
                    if q < QUARTERS - 1:
                        act.dma_start(gate_dram[nxt, q], src).then_inc(gates_stored[q % 2], 16)
                    else:
                        act.dma_start(gate_dram[nxt, q, :, 0:EARLY, :], src[:, 0:EARLY, :]).then_inc(gates_early, 16)

                def staging_free(q):
                    Q = 4 * nxt + q
                    if Q >= 2:
                        act.wait_ge(gates_stored[q % 2], 16 * (Q // 2))
                    if q == 1:
                        after(act, gates_early, 16 * nxt)

                def body(i, q=None, first=False, opens=False, last=False):
                    for t in range(4):
                        k = 4 * i + (t + P * n)
                        behind = n >= 0 and not (first and t == 0)
                        if behind:
                            gelu(k - 1, t + 3)
                        if q is not None:
                            if t:
                                if opens and t == 1:
                                    staging_free(q)
                                copy_gates(i, q, t - 1)
                            elif not opens:
                                copy_gates(i - 1, q, 3)
                            elif q:
                                copy_gates(i - 1, q - 1, 3)
                                flush(q - 1)
                        if behind:
                            split_coef(k - 1, t + 3)
                        if n >= 0:
                            if not (last and t == 3):
                                split_u(k + 1, i, n, t + 1)
                            split_v(k, t)
                        if first:
                            if t == 1:
                                act.dma_start(gate_dram[n, QUARTERS - 1, :, EARLY:, :], staged[:, 1, EARLY:, :]
                                              ).then_inc(gates_stored[1], 16)
                            if n and t:
                                norm_y(n - 1, t)

                if n >= 0:
                    if n == 0:
                        split_u(0, 0, 0, 0)
                    body(0, first=True)
                    with act.Fori(1, 16) as i:
                        body(i)
                if nxt is not None:
                    act.wait_ge(shifted, nxt + 1)
                    A(sel[:, 2, :], sel[:, 2, :], ACT.Exp).then_inc(exped, 1)
                    act.wait_ge(sel_turned, nxt + 1)
                    turned_ = ps[:, 2:4, 0:3 * P].rearrange("p b (x n) -> p x b n", x=3)
                    for x in range(3):
                        last = copy(sel_t[:, x, :].rearrange("p (b n) -> p b n", b=2), turned_[:, x])
                    last = copy(gate_hi[:].rearrange("p (b n) -> p b n", b=2), turned_[:, 2])
                    last.then_inc(sel_copied, 1)
                    for q in range(QUARTERS):
                        body(16 + 4 * q, q=q, opens=True)
                        with act.Fori(17 + 4 * q, 20 + 4 * q) as i:
                            body(i, q=q)
                    copy_gates(31, QUARTERS - 1, 3)
                    flush(QUARTERS - 1)
                else:
                    with act.Fori(16, 31) as i:
                        body(i)
                    body(31, last=True)
                if n >= 0:
                    gelu(P * (n + 1) - 1, 3)
                    split_coef(P * (n + 1) - 1, 3)
                if nxt is not None:
                    act.wait_ge(h_in, 16 * (nxt + 1))
                    after(act, s_done, P * nxt)
                    copy(flat(h_hi[:]), flat(f_y[:])).then_inc(h_hi_ready, 1)
            for part in range(1, 4):
                norm_y(PASSES - 1, part)

        @block.vector
        def _(dve):
            V = nc.vector
            tt, ts, stt = V.tensor_tensor, V.tensor_scalar, V.scalar_tensor_tensor
            iota16 = iota[:, 0:TOPK]
            square = (P, TOPK, TOPK)

            def flat(t):
                return t.rearrange("p a b -> p (a b)")

            def top16(src, spare_, val, idx):
                V.max(val[:, 0:8], src)
                dve.drain()
                V.max_index(idx[:, 0:8], val[:, 0:8], src)
                last = V.match_replace(spare_, val[:, 0:8], src, NEG)
                dve.drain()
                V.max(val[:, 8:16], spare_)
                dve.drain()
                V.max_index(idx[:, 8:16], val[:, 8:16], spare_)
                return last

            def search(nxt, i, part):
                if part == 0:
                    dve.wait_ge(score_loaded[nxt], 16 * i + 16)
                    V.tensor_copy(jf[:, 0, 0:1], score_in[:, 0, 0:1])
                    dve.drain()
                if part < 2:
                    top16(score_in[:, part, :], cand[:, part].rearrange("p a b -> p (a b)")[:, 0:P], best[:, part, :], besti[:, part, :])
                    if part == 1:
                        dve.drain()
                        V.tensor_copy(bestf[:], besti[:]).then_inc(score_free, 1)
                    dve.drain()
                elif part == 2:
                    tt(cand[:, 0], best[:, 0, :].unsqueeze(2).broadcast_to(square),
                       best[:, 1, :].unsqueeze(1).broadcast_to(square), ALU.add)
                    dve.drain()
                    top16(flat(cand[:, 0]), flat(cand[:, 1]), pair[:], jbest[:])
                    dve.drain()
                    ts(jhalf[:, 0, :], jbest[:], 4, None, ALU.logical_shift_right)
                    ts(jhalf[:, 1, :], jbest[:], TOPK - 1, None, ALU.bitwise_and)
                    dve.drain()
                    V.tensor_copy(jf[:], jhalf[:])
                    dve.drain()
                else:
                    V.tensor_copy(sel[:, 2, bass.ds(16 * i, TOPK)], pair[:])
                    for x in range(2):
                        tt(cand[:, x], jf[:, x, :].unsqueeze(2).broadcast_to(square),
                           iota16.unsqueeze(1).broadcast_to(square), ALU.is_equal)
                    dve.drain()
                    for x in range(2):
                        tt(cand[:, x], cand[:, x], bestf[:, x, :].unsqueeze(1).broadcast_to(square), ALU.mult)
                    dve.drain()
                    for x in range(2):
                        V.tensor_reduce(sel[:, x, bass.ds(16 * i, TOPK)], cand[:, x], AX.X, ALU.add)
                    dve.drain()

            dve.wait_ge(consts_in, 32)
            cs = par[:, V_C:V_C + 16].rearrange("p (k g) -> p k g", g=2)
            lamv = par[:, V_LAM:V_LAM + 256].rearrange("p (m k n) -> p m k n", m=2, k=2)
            tt(rtmp[:, 0:128].rearrange("p (m n) -> p m n", m=2), lamv[:, :, 0, :], lamv[:, :, 1, :], ALU.mult)
            dve.drain()
            V.tensor_reduce(small[:, 0:2], rtmp[:, 0:128].rearrange("p (m n) -> p m n", m=2), AX.X,
                            ALU.add).then_inc(lam_dot, 1)
            dve.wait_ge(silu_a, 1)
            tt(silu_c[:], silu_c[:], cs, ALU.mult).then_inc(silu_b, 1)
            dve.wait_ge(lam_exp, 1)
            stt(out=nlam[:], in0=small[:, 3:4], scalar=-LAM_INIT, in1=small[:, 2:3], op0=ALU.add, op1=ALU.subtract)
            ts(gsub[:], par[:, V_GSUB:V_GSUB + 1], 1.0 - LAM_INIT, None, ALU.mult)

            def finish_mod(bank, c0, c1, n, v):
                tt(mod[:, c0:c1, :], ps[:, bank, 2 * c0:2 * c1].rearrange("p (c g) -> p c g", g=2),
                   par[:, V_BADA + c0:V_BADA + c1].unsqueeze(2).broadcast_to((P, c1 - c0, 2)),
                   ALU.add).then_inc(mod_ready, 1)
                dve.drain()
                for g in range(2):
                    stt(out=scl[:, g, n, :], in0=mod[:, 24 * n + 8:24 * n + 16, g], scalar=1.0,
                        in1=par[:, v:v + 8], op0=ALU.add, op1=ALU.mult)

            dve.wait_ge(ada_done, ADA_FIRST)
            finish_mod(0, 0, 4 * ADA_FIRST, 0, V_G1)

            for g, S in enumerate(SEQS):
                B = S // P
                nsq = 2 * KC * g
                if g:
                    all_done(dve)

                def inverse(dst, src, n):
                    ts(dst, src, 1.0 / n, EPS, ALU.mult, ALU.add)
                    dve.drain()
                    return V.reciprocal(dst, dst)

                def norm(n, dst):
                    dve.wait_ge(sq_summed, nsq + KC * (n + 1))
                    inverse(rstd[:, 0:S], ps[:, 2, 0:S], D).then_inc(var_ready, 1)
                    dve.wait_ge(rstd_ready, 2 * g + n + 1)
                    for c in range(KC):
                        stt(out=dst[:, c, 0:S], in0=hbuf[:, c, 0:S], scalar=scl[:, g, n, c:c + 1],
                            in1=rstd[:, 0:S], op0=ALU.mult, op1=ALU.mult).then_inc(scaled, 1)
                    if n == 0:
                        dve.drain()
                        for c in range(KC):
                            dve.wait_ge(n_rounded, KC * g + c + 1)
                            stt(out=n_lo[:, c, 0:S], in0=hbuf[:, c, 0:S], scalar=mod[:, c, g:g + 1],
                                in1=n_hi[:, c, 0:S].bitcast(F32), op0=ALU.add, op1=ALU.subtract).then_inc(n_split, 1)

                norm(0, hbuf)

                def head_variance(m):
                    dve.wait_ge(o_summed, m + (8 * g + 1))
                    v = ovar[:, bass.ds(m, 1), 0:S].rearrange("p a s -> p (a s)")
                    inverse(v, ps[:, 6, 0:S], P).then_inc(o_var, 1)

                def head(h, par_, do_proj, do_att):
                    hg = 8 * g + h
                    q0 = qbase[g] + (h - 1) * B

                    def maxima(j):
                        pe_ = j % 2
                        nm = small[:, 4 + 2 * pe_:6 + 2 * pe_]
                        dve.wait_ge(scored, q0 + j + 1)
                        V.tensor_reduce(nm, ps[:, 3:5, 0:S], AX.X, ALU.max)
                        dve.drain()
                        ts(nm, nm, -HALF ** -0.5, None, ALU.mult).then_inc(maxed, 1)

                    def mix(j):
                        pe_ = j % 2
                        zs = small[:, 8 + 2 * pe_:10 + 2 * pe_]
                        dve.wait_ge(expd_ready, q0 + j + 1)
                        after(dve, turned, q0 + j - 1)
                        V.reciprocal(zs, zs)
                        dve.drain()
                        ts(expd[:, pe_, 1, 0:S], expd[:, pe_, 1, 0:S], zs[:, 1:2], nlam[:, 0:1], ALU.mult, ALU.mult)
                        dve.drain()
                        stt(out=amix[:, pe_, 0:S], in0=expd[:, pe_, 0, 0:S], scalar=zs[:, 0:1],
                            in1=expd[:, pe_, 1, 0:S], op0=ALU.mult, op1=ALU.add).then_inc(mixed, 1)

                    def rope_(x, i):
                        dst = qk[:, par_, i, 0:S]
                        dve.wait_ge(copied[x], hg + 1)
                        after(dve, scored, q0)
                        tt(dst, qkraw[:, i, 0:S], cossin[:, 0, 0:S], ALU.mult)
                        dve.wait_ge(rotated[x], hg + 1)
                        tt(rtmp[:, 0:S], ps[:, 2, 0:S], cossin[:, 1, 0:S], ALU.mult)
                        dve.drain()
                        tt(dst, dst, rtmp[:, 0:S], ALU.add).then_inc(roped[x], 1)

                    if do_att:
                        maxima(0)
                        mix(0)
                        maxima(1)
                        mix(1)
                        if B > 2:
                            maxima(2)
                    if do_proj:
                        rope_("q", 0)
                    if do_att and B > 2:
                        mix(2)
                        maxima(3)
                    if do_proj:
                        rope_("k", 1)
                    if do_att:
                        if B > 2:
                            mix(3)
                        if not isinstance(h, int) or h >= 2:
                            head_variance(h - 2)

                head(0, 0, True, False)
                head(1, 1, True, True)
                with dve.Fori(0, HEADS // 2 - 1) as i:
                    head(2 * i + 2, 0, True, True)
                    head(2 * i + 3, 1, True, True)
                if g == 0:
                    dve.wait_ge(ada_done, UNITS_ADA)
                    finish_mod(7, 4 * ADA_FIRST, 4 * UNITS_ADA, 1, V_G2)
                head(HEADS, 0, False, True)

                for h in range(HEADS):
                    if h == HEADS // 2:
                        head_variance(HEADS - 1)
                    if h % (HEADS // 2) == 0:
                        dve.wait_ge(o_rstd, 2 * g + h // (HEADS // 2) + 1)
                    stt(out=obuf[:, h, 0:S], in0=obuf[:, h, 0:S], scalar=gsub[:, 0:1], in1=ovar[:, h, 0:S],
                        op0=ALU.mult, op1=ALU.mult).then_inc(o_normed, 1)
                def branches(c, j):
                    z = zbuf[:, bass.ds(c, 1), 0:S].rearrange("p a s -> p (a s)")
                    att = expd[:, j, 1, 0:S]
                    dve.wait_ge(sig_done, c + (8 * g + 1))
                    tt(z, ps[:, zbanks[j][3], 0:S], expd[:, j, 0, 0:S], ALU.mult)
                    tt(att, ps[:, zbanks[j][2], 0:S], att, ALU.mult)
                    dve.drain()
                    tt(z, z, att, ALU.add).then_inc(z_ready, 1)

                with dve.Fori(0, KC // 2 - 1) as i:
                    for j in range(2):
                        branches(2 * i + j, j)
                        if g:
                            for x in range(1 + j):
                                for part in range(4):
                                    search(0, 3 * i + (j + x), part)
                branches(KC - 2, 0)
                if g:
                    for part in range(4):
                        search(0, Z_SEARCHES - 1, part)
                branches(KC - 1, 1)
                dve.wait_ge(x_again, 16 * (g + 1))
                for c in range(KC):
                    dve.wait_ge(out_done, 8 * g + c + 1)
                    stt(out=hbuf[:, c, 0:S], in0=ps[:, c % 2, 0:S], scalar=mod[:, 16 + c, g:g + 1],
                        in1=obuf[:, c, 0:S], op0=ALU.mult, op1=ALU.add).then_inc(x1_ready, 1)
                for k in range(KC):
                    last = ts(diag[:, k, :], ident, mod[:, 40 + k, g:g + 1], None, ALU.mult)
                last.then_inc(diag_ready, 1)
                dve.drain()
                norm(1, obuf)
                if g:
                    with dve.Fori(Z_SEARCHES, 16) as i:
                        for part in range(4):
                            search(0, i, part)

            all_done(dve)

            four = (P, 4, P)

            def each(per_token, tok):
                return per_token[:, bass.ds(tok, 4)].unsqueeze(2).broadcast_to(four)

            def hot_keys(s, tok, t, whole):
                j = t % 2
                after(dve, hot2l_ready, s - 1)
                tt(hot2[:, j], each(sel_t[:, 1, :], tok), iota.unsqueeze(1).broadcast_to(four),
                   ALU.is_equal).then_inc(hot2_ready, 1)
                after(dve, g_done, s - 1)
                last = tt(hot1[:, j], each(sel_t[:, 0, :], tok), iota.unsqueeze(1).broadcast_to(four), ALU.is_equal)
                if whole:
                    last.then_inc(hot2h_ready, 1)

            def hot_gates(tok, t):
                dve.drain()
                tt(hot2h[:, t % 2], hot2[:, t % 2], each(gate_hi[:].bitcast(F32), tok), ALU.mult).then_inc(hot2h_ready, 1)

            def split_u(k, t):
                dve.wait_ge(u_hi_ready, k + 1)
                tt(flat(u_lo[:, t % 2]), raw[:, t % 4, 0:D], flat(u_hi[:, t % 2].bitcast(F32)),
                   ALU.subtract).then_inc(u_lo_ready, 1)

            def coefficient(k, loaded, t):
                dve.wait_ge(gelu_done, k + 1)
                dve.wait_ge(gate_loaded[t % 4 // 2], loaded)
                c = coef[:, t % 2, :].rearrange("p (q s) -> p q s", q=QUARTERS)
                tt(c, c, gate_in[:, t % 4 // 2, :, t % 2, :], ALU.mult).then_inc(coef_ready, 1)

            def split_coef(k, t):
                dve.wait_ge(c_hi_ready, k + 1)
                tt(c_lo[:, t % 2, :], coef[:, t % 2, :], c_hi[:, t % 2, :].bitcast(F32),
                   ALU.subtract).then_inc(c_lo_ready, 1)

            def norm_y(n, part):
                if part == 1:
                    tt(f_y[:], f_y[:], f_x1[:], ALU.add).then_inc(y_ready, 1)
                elif part == 2:
                    dve.wait_ge(y_squared, n + 1)
                    inverse(small[:, 14:16], small[:, 12:14], D).then_inc(y_var, 1)
                else:
                    dve.wait_ge(y_rstd, n + 1)
                    for j in range(2):
                        stt(out=f_y[:, j, :], in0=f_y[:, j, :], scalar=small[:, 14 + j:15 + j], in1=f_gf[:],
                            op0=ALU.mult, op1=ALU.mult).then_inc(y_final, 1)

            for n in range(-1, PASSES):
                nxt = n + 1 if n + 1 < PASSES else None

                def body(i, searching=False, building=False, first=False, last=False):
                    for t in range(4):
                        k = 4 * i + (t + P * n)
                        tok = 16 * i + (4 * t - 256)
                        behind = n >= 0 and not (first and t == 0)
                        if behind:
                            coefficient(k - 1, 16 * i + (16 * (P // 4) * n + (16 if t else 0)), t + 3)
                        if building:
                            hot_keys(4 * i + (STEPS * (nxt - 1) + t), tok, t, whole=n < 0)
                        if behind:
                            split_coef(k - 1, t + 3)
                        if building and n >= 0:
                            hot_gates(tok, t)
                        if searching:
                            search(nxt, i, t)
                        if n >= 0 and not (last and t == 3):
                            split_u(k + 1, t + 1)
                        if first and n and t:
                            norm_y(n - 1, t)

                if n >= 0:
                    if n == 0:
                        split_u(0, 0)
                    body(0, searching=nxt is not None, first=True)
                    with dve.Fori(1, 16) as i:
                        body(i, searching=nxt is not None)
                if nxt is not None:
                    v = sel[:, 2, :].rearrange("p (h k) -> p h k", k=TOPK)
                    per_head = gsum[:].unsqueeze(2).broadcast_to(square)
                    V.tensor_copy(gsum[:], v[:, :, 0])
                    dve.drain()
                    tt(v, v, per_head, ALU.subtract).then_inc(shifted, 1)
                    dve.wait_ge(exped, nxt + 1)
                    V.tensor_reduce(gsum[:], v, AX.X, ALU.add)
                    dve.drain()
                    V.reciprocal(gsum[:], gsum[:])
                    dve.drain()
                    tt(v, v, per_head, ALU.mult).then_inc(sel_ready, 1)
                    dve.wait_ge(sel_copied, nxt + 1)
                    if n >= 0:
                        tt(gate_lo, sel_t[:, 2, :], gate_hi[:].bitcast(F32), ALU.subtract)
                        dve.drain()
                    body(16, building=True)
                    with dve.Fori(17, 32) as i:
                        body(i, building=True)
                else:
                    with dve.Fori(16, 31) as i:
                        body(i)
                    body(31, last=True)
                if n >= 0:
                    coefficient(P * (n + 1) - 1, 16 * (P // 4) * (n + 1), 3)
                    split_coef(P * (n + 1) - 1, 3)
                if nxt is not None:
                    dve.wait_ge(h_hi_ready, nxt + 1)
                    tt(flat(h_lo[:]), flat(f_y[:]), flat(h_hi[:].bitcast(F32)), ALU.subtract).then_inc(h_lo_ready, 1)
                if n >= 0:
                    dve.wait_ge(v_done, P * (n + 1))
                    dve.wait_ge(fin_in, 16 + 48 * (n + 1))
                    dve.drain()
                    for j in range(2):
                        last = tt(f_y[:, j, :].rearrange("p (a n) -> p a n", a=2), ps[:, 4 + 2 * j:6 + 2 * j, :],
                                  f_gt2[:].rearrange("p (a n) -> p a n", a=2), ALU.mult)
                    last.then_inc(acc_read, 1)
                    dve.drain()
            for part in range(1, 4):
                norm_y(PASSES - 1, part)

        @block.gpsimd
        def _(pool):
            G = nc.gpsimd
            for g, S in enumerate(SEQS):
                if g:
                    all_done(pool)
                L = S + 2 * PAD
                G.memset(pbuf[:, :, 0:PAD], 0.0)
                G.memset(pbuf[:, :, PAD + S:L], 0.0)

                def lower(n, j, u, i):
                    pool.wait_ge(w_hi_ready, n + (SPLIT_TILES * g + 1))
                    o = (u % 2) * UNIT + i * TILE
                    G.tensor_tensor(w_lo[:, j, :], ring[:, o:o + TILE], w_hi[:, j, :].bitcast(F32), ALU.subtract
                                    ).then_inc(w_lo_ready, 1)

                def window(c, w):
                    pool.wait_ge(p_copied, 4 * g + c + 1)
                    src, lo = pbuf[:, c, :], 0
                    for n in range(c + 1):
                        d = max(1, 2 ** n // 2)
                        dst = ptmp[:, n % 2, :]
                        lo, back, ahead = (1, 1, 0) if n == 0 else (lo + d, d, d)
                        pool.drain()
                        G.tensor_tensor(dst[:, lo:L - lo], src[:, lo - back:L - lo - back],
                                        src[:, lo + ahead:L - lo + ahead], ALU.add)
                        src = dst
                    pool.drain()
                    mean = src[:, PAD:PAD + S]
                    G.tensor_scalar(mean, mean, 1.0 / w, None, ALU.mult)
                    pool.drain()
                    G.tensor_tensor(mean[:, 0:PAD], mean[:, 0:PAD], edge[:, c, 0:PAD], ALU.mult)
                    G.tensor_tensor(mean[:, S - PAD:S], mean[:, S - PAD:S], edge[:, c, PAD:2 * PAD], ALU.mult)
                    pool.drain()
                    G.tensor_tensor(pdif[:, c, 0:S], mean, pbuf[:, c, PAD:PAD + S], ALU.subtract).then_inc(pool_diff, 1)

                def head_weights(h, par_):
                    for i in range(3):
                        lower(3 * h + (4 + i), i, b + 1 + par_, i)

                b = ubase[g]
                for c in range(4):
                    lower(c, 1 + c % 2, b, c)
                for h in range(4):
                    head_weights(h, h % 2)
                    window(h, WINDOWS[h])
                with pool.Fori(2, HEADS // 2) as i:
                    for j in range(2):
                        head_weights(2 * i + j, j)
                if g:
                    load_scores(pool, 0, 0)
                for c in range(KC):
                    for m in range(2):
                        lower(4 + 3 * HEADS + 2 * c + m, 2 if (c, m) == (1, 0) else m, b + 9 + c, m)
                    if g and c >= 2:
                        for x in range(1 + c % 2):
                            load_scores(pool, 0, 3 * (c // 2 - 1) + 1 + c % 2 + x)
            with pool.Fori(Z_SEARCHES, 16) as i:
                load_scores(pool, 0, i)

            all_done(pool)
            for n in range(-1, PASSES):
                nxt = n + 1 if n + 1 < PASSES else None

                def body(i, building=False):
                    for t in range(4):
                        if building:
                            s = 4 * i + (STEPS * (nxt - 1) + t)
                            after(pool, g_done, s - 1)
                            pool.wait_ge(hot2_ready, s + 1)
                            lo = gate_lo[:, bass.ds(16 * i + (4 * t - 256), 4)]
                            dst = hot2l[:, t % 2] if n >= 0 else hot2g[:, t % 2]
                            G.tensor_tensor(dst, hot2[:, t % 2], lo.unsqueeze(2).broadcast_to((P, 4, P)),
                                            ALU.mult).then_inc(hot2l_ready, 1)
                        if n >= 0:
                            pool.wait_ge(v_hi_ready, 4 * i + (P * n + t + 1))
                            G.tensor_tensor(v_lo[:, t % 2, :], raw[:, t, D:2 * D], v_hi[:, t % 2, :].bitcast(F32),
                                            ALU.subtract).then_inc(v_lo_ready, 1)

                if n >= 0:
                    with pool.Fori(0, 16) as i:
                        body(i)
                if nxt is not None:
                    body(16, building=True)
                    with pool.Fori(17, 32) as i:
                        body(i, building=True)
                else:
                    with pool.Fori(16, 32) as i:
                        body(i)


def shape_constants():
    c = np.zeros((P, C_N), np.float32)
    c[:, C_ID:C_ID + P] = np.eye(P)
    c[:, C_ONE:C_ONE + P] = 1
    for i in range(P):
        if i % HALF < HALF // 2:
            c[i + HALF // 2, C_ROT + i] = -1
        else:
            c[i - HALF // 2, C_ROT + i] = 1
    c[:, C_IOTA:C_IOTA + P] = np.arange(P)
    for n, w in enumerate(WINDOWS):
        for i in range(PAD):
            c[:, C_EDGE + 16 * n + i] = w / (min(i + w // 2, SMAX) - max(i - w // 2, 0))
            back = PAD - i
            c[:, C_EDGE + 16 * n + PAD + i] = w / (min(w // 2, back) + w // 2)
    inv = (1.0 / (10000.0 ** (np.arange(0, HALF, 2, dtype=np.float32) / HALF))).astype(np.float32)
    ang = np.arange(SMAX, dtype=np.float32)[None, :] * np.tile(inv, 4)[:, None]
    rope = np.stack([np.cos(ang), np.sin(ang)], axis=1).astype(np.float32)
    return c, rope


def kernel(**inputs):
    import concourse.bacc as _bacc
    from concourse.bass_utils import run_bass_kernel_spmd as _run

    a = {k: np.asarray(v) for k, v in inputs.items()}
    f = np.float32

    def tiles(w):
        r, n = w.shape
        return w.reshape(r // P, P, n // P, P).transpose(2, 1, 0, 3)

    units = np.zeros((UNITS_ADA + UNITS_GROUP, P, 4, KC, P), f)
    units[:UNITS_ADA] = tiles(a["w_ada"][0]).reshape(UNITS_ADA, 4, P, KC, P).transpose(0, 2, 1, 3, 4)
    u = units[UNITS_ADA:]
    w_in = tiles(a["w_in"][0])
    gate, att, out_, peer = (tiles(a[k][0]) for k in ("w_gate", "w_att_out", "w_out", "w_peer_q"))
    po = tiles(a["w_pool_out"][0])
    for i in range(4):
        u[0][:, i] = w_in[i]
    for h in range(HEADS):
        for i in range(3):
            u[1 + h][:, i] = w_in[4 + 8 * i + h]
    for c in range(KC):
        u[9 + c][:, 0], u[9 + c][:, 1], u[9 + c][:, 2] = gate[c], gate[KC + c], att[c]
        u[9 + c][:, 3, 0:4] = po[c]
        u[17 + c // 4][:, c % 4] = out_[c]
        u[19 + c // 4][:, c % 4] = peer[c]

    def cols(v):
        return v.reshape(-1, P).T

    params = np.zeros((P, V_N), f)
    for at, v in ((V_G1, a["g_norm1"]), (V_G2, a["g_norm2"]), (V_BADA, a["b_ada"]), (V_BGATE, a["b_gate"]),
                  (V_PSC, a["pool_scale"]), (V_GSUB, a["g_sub"])):
        c = cols(v[0])
        params[:, at:at + c.shape[1]] = c
    cc = np.stack([a["c_prompt"][0].reshape(KC, P), a["c_sample"][0].reshape(KC, P)], axis=2)
    params[:, V_C:V_C + 16] = cc.transpose(1, 0, 2).reshape(P, 16)
    params[:, V_LAM:] = np.concatenate([a[k][0] for k in ("lam_q1", "lam_k1", "lam_q2", "lam_k2")])[None, :]
    keys = np.zeros((P, HEADS, 2 * P), f)
    for x in range(2):
        keys[HALF * x:HALF * (x + 1), :, P * x:P * (x + 1)] = a["peer_keys"][0][:, x].transpose(2, 0, 1)
    consts, rope = shape_constants()
    x_t = [a[k][0].T.reshape(KC, P, -1).transpose(1, 0, 2) for k in ("x_prompt", "x_sample")]
    eu = a["peer_u"][0].reshape(P, P, KC, P).transpose(1, 3, 2, 0).reshape(P, P, D)
    ev = a["peer_v"][0].reshape(P, P, D).transpose(1, 0, 2)
    sent = {
        "consts": consts, "params": params, "rope": rope, "keys": keys,
        "pool_w": a["pool_w"][0].transpose(1, 0, 2), "g_final": np.broadcast_to(a["g_final"], (P, D)),
        "x_t0": x_t[0], "x_t1": x_t[1], "weights": units.reshape(-1, P, UNIT),
        "table": np.concatenate([eu, ev], axis=2),
    }
    sent = {"in_" + k: np.ascontiguousarray(v) for k, v in sent.items()}
    nc = _bacc.Bacc("TRN2", target_bir_lowering=False, num_devices=1)
    ap = {k: nc.dram_tensor(k, v.shape, mybir.dt.from_np(v.dtype), kind="ExternalInput").ap() for k, v in sent.items()}
    outs = [nc.dram_tensor("out_%d" % g, (1, S, D), F32, kind="ExternalOutput").ap() for g, S in enumerate(SEQS)]
    build(nc, ap["in_consts"], ap["in_params"], ap["in_rope"], ap["in_keys"], ap["in_pool_w"], ap["in_g_final"],
          [ap["in_x_t0"], ap["in_x_t1"]], ap["in_weights"], ap["in_table"], outs)
    r = _run(nc, [sent], core_ids=[0])
    return tuple(r.results[0]["out_%d" % g] for g in range(2))
```
